# Optimizing a Trainium2 kernel written in Bass

```python
import jax, jax.numpy as jnp
from jax import lax
import numpy as np

D_MODEL = 1024
BATCH = 1
SEQ = 512
DEPTH = 2
DEC_BATCH = 8
DEC_SEQ = 8
PAST_LEN = 512
PAGE_SIZE = 128

N_HEADS = 16
HEAD_DIM = D_MODEL // N_HEADS
N_A_LAYERS = DEPTH // 2
N_B_LAYERS = DEPTH - N_A_LAYERS
CONV_A_WIDTH = 31
FFN_CONV_WIDTH = 3
D_FF = ((8 * D_MODEL // 3 + 255) // 256) * 256
Q_BLOCK = 128
EPS = 1e-6
SB_BIAS_INIT = -7.0

kernel_name = 'yoco_conformer_stickbreak_decoder_step'

def rmsnorm(x, g):
    xf = x.astype(jnp.float32)
    y = xf * lax.rsqrt(jnp.mean(xf * xf, axis=-1, keepdims=True) + EPS)
    return (y * g.astype(jnp.float32)).astype(x.dtype)

def layernorm(x, g, b):
    xf = x.astype(jnp.float32)
    mu = jnp.mean(xf, axis=-1, keepdims=True)
    var = jnp.mean(jnp.square(xf - mu), axis=-1, keepdims=True)
    y = (xf - mu) * lax.rsqrt(var + EPS)
    return (y * g.astype(jnp.float32) + b.astype(jnp.float32)).astype(x.dtype)

def modulated_rmsnorm(x, g, shift, scale):
    return rmsnorm(x, g) * (1 + scale[:, None, :]) + shift[:, None, :]

def causal_depthwise_conv(x, buf, w, b):
    width, ch = w.shape
    xp = jnp.concatenate([buf.astype(x.dtype), x], axis=1)
    y = lax.conv_general_dilated(xp, w[:, None, :].astype(x.dtype), window_strides=(1,), padding='VALID',
                                 dimension_numbers=('NWC', 'WIO', 'NWC'), feature_group_count=ch)
    return y + b, xp[:, -(width - 1):, :]

def conformer_conv(h, buf, w_in, w_dw, b_dw, ln_g, ln_b, w_out):
    a, gate = jnp.split(h @ w_in, 2, axis=-1)
    u = a * jax.nn.sigmoid(gate)
    u, tail = causal_depthwise_conv(u, buf, w_dw, b_dw)
    u = layernorm(u, ln_g, ln_b)
    return jax.nn.silu(u) @ w_out, tail

def conv_ffn(h, buf, w_up, w_dw, b_dw, w_down):
    g, val = jnp.split(h @ w_up, 2, axis=-1)
    g, tail = causal_depthwise_conv(g, buf, w_dw, b_dw)
    return (jax.nn.gelu(g) * val) @ w_down, tail

def _sb_block(q, k, v, bias, q_pos, k_pos):
    z = jnp.einsum('bqhd,bkhd->bhqk', q, k).astype(jnp.float32) * (HEAD_DIM ** -0.5)
    z = z + bias.astype(jnp.float32)[None, :, None, None]
    causal = k_pos[None, :] < q_pos[:, None]
    log_1m = jnp.where(causal, jax.nn.log_sigmoid(-z), 0.0)
    suffix = lax.cumsum(log_1m, axis=3, reverse=True) - log_1m
    att = jnp.where(causal, jnp.exp(jax.nn.log_sigmoid(z) + suffix), 0.0)
    return jnp.einsum('bhqk,bkhd->bqhd', att.astype(v.dtype), v)

def stick_breaking_attention(q, k, v, bias, q_offset):
    t_q = q.shape[1]
    outs = []
    for start in range(0, t_q, Q_BLOCK):
        end = min(start + Q_BLOCK, t_q)
        k_end = q_offset + end
        q_pos = q_offset + jnp.arange(start, end)
        k_pos = jnp.arange(k_end)
        outs.append(_sb_block(q[:, start:end], k[:, :k_end], v[:, :k_end], bias, q_pos, k_pos))
    return jnp.concatenate(outs, axis=1)

def trunk(x, c, conv_a_buf, ffn_buf, past_k, past_v, q_offset,
          w_ada, b_ada, g_pre_mix, g_post_mix, g_pre_ffn, g_post_ffn,
          w_a_in, w_a_dw, b_a_dw, ln_a_g, ln_a_b, w_a_out,
          g_kv, w_kv, w_q, w_o, b_sb, w_ffn_up, w_ffn_dw, b_ffn_dw, w_ffn_down):
    bsz, t_new, _ = x.shape
    mod = jnp.einsum('bd,lde->lbe', jax.nn.silu(c), w_ada) + b_ada[:, None, :]
    conv_tails, ffn_tails = [], []
    k_all = v_all = k_new = v_new = None
    for l in range(DEPTH):
        shift_m, scale_m, gate_m, shift_f, scale_f, gate_f = jnp.split(mod[l], 6, axis=-1)
        h = modulated_rmsnorm(x, g_pre_mix[l], shift_m, scale_m)
        if l < N_A_LAYERS:
            y, tail = conformer_conv(h, conv_a_buf[l], w_a_in[l], w_a_dw[l], b_a_dw[l],
                                     ln_a_g[l], ln_a_b[l], w_a_out[l])
            conv_tails.append(tail)
        else:
            j = l - N_A_LAYERS
            q = (h @ w_q[j]).reshape(bsz, t_new, N_HEADS, HEAD_DIM)
            o = stick_breaking_attention(q, k_all, v_all, b_sb[j], q_offset)
            y = o.reshape(bsz, t_new, N_HEADS * HEAD_DIM) @ w_o[j]
        x = x + gate_m[:, None, :] * rmsnorm(y, g_post_mix[l])
        h = modulated_rmsnorm(x, g_pre_ffn[l], shift_f, scale_f)
        y, tail = conv_ffn(h, ffn_buf[l], w_ffn_up[l], w_ffn_dw[l], b_ffn_dw[l], w_ffn_down[l])
        ffn_tails.append(tail)
        x = x + gate_f[:, None, :] * rmsnorm(y, g_post_ffn[l])
        if l == N_A_LAYERS - 1:
            k_flat, v_flat = jnp.split(rmsnorm(x, g_kv) @ w_kv, 2, axis=-1)
            k_new = k_flat.reshape(bsz, t_new, N_HEADS, HEAD_DIM)
            v_new = v_flat.reshape(bsz, t_new, N_HEADS, HEAD_DIM)
            if past_k is None:
                k_all, v_all = k_new, v_new
            else:
                k_all = jnp.concatenate([past_k.astype(k_new.dtype), k_new], axis=1)
                v_all = jnp.concatenate([past_v.astype(v_new.dtype), v_new], axis=1)
    return x, jnp.stack(conv_tails), jnp.stack(ffn_tails), k_new, v_new

def setup_inputs(seed: int = 0) -> dict:
    key = jax.random.key(seed)
    ks = iter(jax.random.split(key, 40))

    def nrm(shape, scale):
        return jax.random.normal(next(ks), shape, jnp.float32) * scale

    def gain(shape):
        return 1.0 + nrm(shape, 0.05)

    n_pages = PAST_LEN // PAGE_SIZE
    n_used = DEC_BATCH * n_pages
    n_phys = n_used + n_used // 4
    page_table = jax.random.permutation(next(ks), n_phys)[:n_used].reshape(DEC_BATCH, n_pages).astype(jnp.int32)
    hd = N_HEADS * HEAD_DIM
    return {
        'x_prompt': nrm((BATCH, SEQ, D_MODEL), 1.0),
        'x_sample': nrm((DEC_BATCH, DEC_SEQ, D_MODEL), 1.0),
        'c_prompt': nrm((BATCH, D_MODEL), 1.0),
        'c_sample': nrm((DEC_BATCH, D_MODEL), 1.0),
        'state_conv_a': nrm((N_A_LAYERS, DEC_BATCH, CONV_A_WIDTH - 1, D_MODEL), 0.5),
        'state_ffn_conv': nrm((DEPTH, DEC_BATCH, FFN_CONV_WIDTH - 1, D_FF), 1.0),
        'cache_k': nrm((n_phys, PAGE_SIZE, N_HEADS, HEAD_DIM), 1.0),
        'cache_v': nrm((n_phys, PAGE_SIZE, N_HEADS, HEAD_DIM), 1.0),
        'page_table': page_table,
        'w_ada': nrm((DEPTH, D_MODEL, 6 * D_MODEL), D_MODEL ** -0.5),
        'b_ada': nrm((DEPTH, 6 * D_MODEL), 0.02),
        'g_pre_mix': gain((DEPTH, D_MODEL)),
        'g_post_mix': gain((DEPTH, D_MODEL)),
        'g_pre_ffn': gain((DEPTH, D_MODEL)),
        'g_post_ffn': gain((DEPTH, D_MODEL)),
        'w_a_in': nrm((N_A_LAYERS, D_MODEL, 2 * D_MODEL), D_MODEL ** -0.5),
        'w_a_dw': nrm((N_A_LAYERS, CONV_A_WIDTH, D_MODEL), CONV_A_WIDTH ** -0.5),
        'b_a_dw': nrm((N_A_LAYERS, D_MODEL), 0.02),
        'ln_a_g': gain((N_A_LAYERS, D_MODEL)),
        'ln_a_b': nrm((N_A_LAYERS, D_MODEL), 0.02),
        'w_a_out': nrm((N_A_LAYERS, D_MODEL, D_MODEL), D_MODEL ** -0.5),
        'g_kv': gain((D_MODEL,)),
        'w_kv': nrm((D_MODEL, 2 * hd), D_MODEL ** -0.5),
        'w_q': nrm((N_B_LAYERS, D_MODEL, hd), 0.5 * D_MODEL ** -0.5),
        'w_o': nrm((N_B_LAYERS, hd, D_MODEL), hd ** -0.5),
        'b_sb': SB_BIAS_INIT + nrm((N_B_LAYERS, N_HEADS), 0.1),
        'w_ffn_up': nrm((DEPTH, D_MODEL, 2 * D_FF), D_MODEL ** -0.5),
        'w_ffn_dw': nrm((DEPTH, FFN_CONV_WIDTH, D_FF), FFN_CONV_WIDTH ** -0.5),
        'b_ffn_dw': nrm((DEPTH, D_FF), 0.02),
        'w_ffn_down': nrm((DEPTH, D_FF, D_MODEL), D_FF ** -0.5),
    }

def reference(x_prompt, x_sample, c_prompt, c_sample, state_conv_a, state_ffn_conv, cache_k, cache_v, page_table,
              w_ada, b_ada, g_pre_mix, g_post_mix, g_pre_ffn, g_post_ffn,
              w_a_in, w_a_dw, b_a_dw, ln_a_g, ln_a_b, w_a_out,
              g_kv, w_kv, w_q, w_o, b_sb, w_ffn_up, w_ffn_dw, b_ffn_dw, w_ffn_down):
    n_prompt = x_prompt.shape[0]
    conv_a_zero = jnp.zeros((N_A_LAYERS, n_prompt, CONV_A_WIDTH - 1, D_MODEL), x_prompt.dtype)
    ffn_zero = jnp.zeros((DEPTH, n_prompt, FFN_CONV_WIDTH - 1, D_FF), x_prompt.dtype)
    y_prompt, conv_a_prompt, ffn_conv_prompt, k_prompt, v_prompt = trunk(
        x_prompt, c_prompt, conv_a_zero, ffn_zero, None, None, 0,
        w_ada, b_ada, g_pre_mix, g_post_mix, g_pre_ffn, g_post_ffn,
        w_a_in, w_a_dw, b_a_dw, ln_a_g, ln_a_b, w_a_out,
        g_kv, w_kv, w_q, w_o, b_sb, w_ffn_up, w_ffn_dw, b_ffn_dw, w_ffn_down)
    n_seq, n_pages = page_table.shape
    past_len = n_pages * PAGE_SIZE
    past_k = cache_k[page_table].reshape(n_seq, past_len, N_HEADS, HEAD_DIM)
    past_v = cache_v[page_table].reshape(n_seq, past_len, N_HEADS, HEAD_DIM)
    y_sample, conv_a_sample, ffn_conv_sample, k_sample, v_sample = trunk(
        x_sample, c_sample, state_conv_a, state_ffn_conv, past_k, past_v, past_len,
        w_ada, b_ada, g_pre_mix, g_post_mix, g_pre_ffn, g_post_ffn,
        w_a_in, w_a_dw, b_a_dw, ln_a_g, ln_a_b, w_a_out,
        g_kv, w_kv, w_q, w_o, b_sb, w_ffn_up, w_ffn_dw, b_ffn_dw, w_ffn_down)
    return (y_prompt, y_sample, conv_a_prompt, conv_a_sample, ffn_conv_prompt, ffn_conv_sample,
            k_prompt, v_prompt, k_sample, v_sample)


_drawn_inputs = setup_inputs


def setup_inputs(seed=0):
    import zlib

    import numpy as np

    out = dict(_drawn_inputs(seed))
    spreads = {}
    factors = {'ln_a_b': 3.499, 'b_ffn_dw': 5.696}
    for name, (base, spread) in spreads.items():
        noise = np.random.default_rng([zlib.crc32(name.encode()), seed]).standard_normal(out[name].shape)
        drawn = base * np.exp(spread * noise) if base else spread * noise
        out[name] = __import__('jax').numpy.asarray(drawn.astype(out[name].dtype))
    for name, factor in factors.items():
        out[name] = (out[name] * factor).astype(out[name].dtype)
    return out
```

```python
from contextlib import ExitStack

import numpy as np

import concourse.bass as bass
from concourse import mybir

F32 = mybir.dt.float32
F32R = mybir.dt.float32r
BF16 = mybir.dt.bfloat16
I32 = mybir.dt.int32
ALU = mybir.AluOpType
ACT = mybir.ActivationFunctionType

P = 128
D = 1024
C = D // P
TP = 512
NS, TS = 8, 8
TT = TP + NS * TS
HALF = TT // 2
NB = 1 + NS
DEPTH = 2
FF = 2816
FC = FF // P
FH = FC // 2
HEADS, HD = 16, 64
PAIRS = HEADS // 2
WA = 31
WF = 3
PAGE = 128
PAGES = 4
N_PHYS = 40
MODS = 6 * C
EPS = 1e-6
KEY_COLS = TP + (TP - 128) + 128 + (TP - 256)
SP_CLAMP = 40.0

A_IN = (0, 8, C)
A_OUT = (16, 4, C)
UP = {(0, 0): (24, 11, C), (0, 1): (54, 11, C), (1, 0): (116, 11, C), (1, 1): (146, 11, C)}
DOWN = {(0, 0): (46, 4, FH), (0, 1): (76, 4, FH), (1, 0): (138, 4, FH), (1, 1): (168, 4, FH)}
KPROJ = (84, 4, C)
VPROJ = (92, 4, C)
QPROJ = (100, 4, C)
OPROJ = (108, 4, C)
UNITS = 176
PHASES = [A_IN, A_OUT, UP[0, 0], DOWN[0, 0], UP[0, 1], DOWN[0, 1], KPROJ, VPROJ, QPROJ, OPROJ,
          UP[1, 0], DOWN[1, 0], UP[1, 1], DOWN[1, 1]]

PAR = {}
_at = 0
for _name, _n in (("g_pre_mix", 2 * C), ("g_post_mix", 2 * C), ("g_pre_ffn", 2 * C), ("g_post_ffn", 2 * C),
                  ("b_a_dw", C), ("ln_a_g", C), ("ln_a_b", C), ("g_kv", C), ("w_a_dw", C * WA),
                  ("b_ffn_dw", 2 * FC), ("w_ffn_dw", 2 * FC * WF), ("b_ada", 2 * MODS)):
    PAR[_name] = _at
    _at += _n
N_PAR = _at

ADA_RING = 5
ADA_FIRST = 2 * C
CONSTS = 16
TAP_STEPS = WA + 1
SEQ_STEPS = 2 * WA + 4
ADA_PER_UNIT = (2 * MODS - ADA_FIRST) // (2 * A_IN[1])


def blocks(unit):
    for base, pairs, k in PHASES:
        if base <= unit < base + 2 * pairs:
            return k
    raise ValueError(unit)


def tiles_before(base):
    return base // 2 - (VPROJ[1] if base > VPROJ[0] else 0)


def trunk_kernel(nc, x_in, c_in, par_in, b_sb_in, w_ada, w_k8, w_down, state_a, state_f,
                 cache_kt, cache_v, page_table, y_out, conv_a_p, conv_a_s, ffn_tails, k_out, v_out):
    with ExitStack() as ctx:
        cursor = [16512]

        def place(name, shape, dtype=F32, at=None):
            size = int(np.prod(shape[1:])) * (2 if dtype == BF16 else 4)
            size = (size + 31) // 32 * 32
            here = cursor[0] if at is None else at[0]
            if at is None:
                cursor[0] += size
            else:
                at[0] += size
                assert at[0] <= at[1], (name, at)
            return nc.alloc_sbuf_tensor_at(name, shape, dtype, offset=here)

        def region(size):
            start = cursor[0]
            cursor[0] += size
            return lambda skip=0: [start + skip, start + size]

        def sem(name):
            return ctx.enter_context(nc.semaphore(name))

        x = place("x", [P, C, TT])
        raw = [place(f"raw{s}", [P, FH * P]) for s in range(2)]
        w_hi = [place(f"w_hi{s}", [P, FH * P], F32R) for s in range(2)]
        w_lo = [place(f"w_lo{s}", [P, FH * P], F32R) for s in range(2)]
        h_hi = place("h_hi", [P, C, TT], F32R)
        h_lo = place("h_lo", [P, C, TT], F32R)
        par = place("par", [P, N_PAR])
        bsb = place("bsb", [P, HEADS])
        bsb_seq = place("bsb_seq", [P, P])
        one_row = place("one_row", [1, P])
        mod = place("mod", [P, DEPTH, MODS, NB])
        a_mod = place("a_mod", [P, C, NB])
        g_mod = place("g_mod", [P, C, NB])
        no_shift = place("no_shift", [P, C, NB])
        mean_w = place("mean_w", [P, P])
        tri = place("tri", [P, P])
        neg_ones = place("neg_ones", [P, P])
        ident = place("ident", [P, P], BF16)
        mask = place("mask", [P, P], BF16)
        mask_new = place("mask_new", [P, NS * TS], BF16)
        eps_col = place("eps_col", [P, 1])
        rs = place("rs", [P, TT])
        pages = place("pages", [1, NS * PAGES], I32)
        c_raw = place("c_raw", [P, C, NB])
        c_act = place("c_act", [P, C, NB])
        y = place("y", [P, C, TT])
        y_at = lambda: [y_off, y_off + C * TT * 4]
        y_off = cursor[0] - C * TT * 4

        wide = region(2 * FH * TT * 4)
        act_hi = place("act_hi", [P, FH, TT], F32R, at := wide())
        act_lo = place("act_lo", [P, FH, TT], F32R, at)
        u_p = place("u_p", [P, C, WA - 1 + TP], at=(at := wide()))
        u_s = place("u_s", [P, C, NS, WA - 1 + TS], at=at)
        ada_w = [place(f"ada_w{s}", [P, C * P], at=at) for s in range(ADA_RING)]
        k_t = place("k_t", [P, PAIRS, TT], at=(at := wide()))
        v_n = place("v_n", [P, 5, D], at=at)
        k_st = place("k_st", [P, TP], at=at)
        q_st = place("q_st", [P, TP], at=at)
        v_st = place("v_st", [P, 4, P], at=at)
        att_new = place("att_new", [64, 2, PAIRS, NS * TS], at=at)
        q_t = place("q_t", [P, PAIRS, TT], at=y_at())

        temp = region(229368 // 32 * 32 - cursor[0])
        at = temp()
        sq = place("sq", [P, 2, TT], at=at)
        hn = place("hn", [P, 2, TT], at=at)
        y_sum = place("y_sum", [P, TT], at=at)
        shared = at[0] - temp()[0]
        mu = place("mu", [P, TT], at=(at := temp(shared)))
        sig = place("sig", [P, TT], at=at)
        odd_taps = place("odd_taps", [P, TP], at=at)
        s_prod = place("s_prod", [P, 2, NS, TS], at=at)
        y_seq = place("y_seq", [P, NS, TS], at=at)
        u_seq = place("u_seq", [P, NS, WA - 1 + TS], at=at)
        w_seq = place("w_seq", [P, WA + 1], at=at)
        g_pad = place("g_pad", [P, WF - 1 + TP], at=(at := temp(shared)))
        g_seq = place("g_seq", [P, NS, WF - 1 + TS], at=at)
        cv = place("cv", [P, TT], at=at)
        val = place("val", [P, TT], at=at)
        ge = place("ge", [P, TT], at=at)
        prod = place("prod", [P, TT], at=at)
        tails = place("tails", [P, FC, (1 + NS) * 2], at=at)
        f_state = place("f_state", [P, FC, NS * 2], at=at)
        at = temp()
        att = [place(f"att{j}", [P, KEY_COLS], at=at) for j in range(2)]
        att_s = place("att_s", [P, PAGES * P], at=at)
        sp_new = place("sp_new", [64, 2, PAIRS, NS * TS], at=at)
        q_bd = place("q_bd", [P, NS, PAIRS, 2 * TS], at=at)
        k_page = [place(f"k_page{s}", [P, PAIRS, PAGE], at=at) for s in range(2)]
        v_page = [place(f"v_page{s}", [P, D], at=at) for s in range(2)]

        ps = ctx.enter_context(nc.psum_tensor("ps", [P, 8, 512], F32))

        def slot(s):
            return ps[:, 2 * s:2 * s + 2, 0:HALF]

        def two(ap):
            return ap.rearrange("p (b t) -> p b t", b=2)

        STAT = 2

        def prm(name, index, count=1):
            return par[:, bass.ds(PAR[name] + index, count)]

        def seq(ap):
            return ap.rearrange("p (s t) -> p s t", s=NS)

        def per_seq(tile, chunk):
            return tile[:, chunk, 1:NB].unsqueeze(2).to_broadcast([P, NS, TS])

        def chunk(tile, n, lo=0, hi=TT):
            return tile[:, bass.ds(n, 1), lo:hi].rearrange("p a t -> p (a t)")

        s_x, s_c, s_par, s_bsb, s_pages, s_state = (
            sem(n) for n in ("x_in", "c_in", "par_in", "bsb_in", "pages_in", "conv_state_in"))
        s_fstate = sem("ffn_state_in")
        s_const = sem("constants")
        w_in = [sem(f"w_in{s}") for s in range(2)]
        s_hi, s_lo, gemm_done = sem("w_hi_made"), sem("w_lo_made"), sem("unit_multiplied")
        slot_free = [sem(f"slot_free{s}") for s in range(2)]
        ada_in = [sem(f"ada_in{s}") for s in range(ADA_RING)]
        c_ready, ada_done, mod_ready, coef_ready = (
            sem(n) for n in ("c_silu", "ada_chunk_done", "mod_ready", "coefficients"))
        sq_ready, sq_used, stat_done, rs_ready, ln_step = (
            sem(n) for n in ("sq_ready", "sq_summed", "stat_done", "rs_ready", "rs_ln"))
        y_sq, y_scaled, y_scaled_s, y_acc, y_normed, x_ready = (
            sem(n) for n in ("y_squared", "y_scaled", "y_scaled_seq", "y_sq_added", "y_normed", "x_ready"))
        hn_x, hn_p, hn_s, h_hi_ready, h_ready = (
            sem(n) for n in ("hn_x", "hn_prompt", "hn_seq", "h_hi_ready", "h_ready"))
        taps, conv_seq, conv_centred, pads_ready = (
            sem(n) for n in ("taps_added", "seq_taps_added", "conv_centred", "pads_zeroed"))
        gate_copied, cv_tap, conv_step, conv_done, gelu_done = (
            sem(n) for n in ("gate_copied", "cv_last_tap", "conv_step", "conv_done", "gelu_done"))
        state_put, tail_saved = sem("state_put"), sem("tail_saved")
        prod_done, act_hi_done, act_ready = sem("prod_done"), sem("act_hi_done"), sem("act_ready")
        v_act, v_dve = sem("v_read_act"), sem("v_read_dve")
        conv_stored, tails_stored, kv_stored, x_stored = (
            sem(n) for n in ("conv_stored", "tails_stored", "kv_stored", "x_stored"))
        q_bd_zero, new_step = sem("q_bd_zeroed"), sem("new_step")
        k_in, v_in = ([sem(f"{n}_page_in{s}") for s in range(2)] for n in "kv")
        k_used, v_used, kq_staged, v_staged = (
            sem(n) for n in ("k_page_used", "v_page_used", "kq_staged", "v_staged"))
        z_done, clamped, exped, lned, sp_done, suffixed, att_done, av_done = (
            sem(n) for n in ("z_done", "z_clamped", "exp_done", "ln_done", "softplus_done", "suffix_added",
                             "att_done", "av_done"))
        seq_bank_free, pair_bank_free, o_hi_done = (
            sem(n) for n in ("seq_bank_free", "pair_bank_free", "o_hi_done"))

        block = ctx.enter_context(nc.Block())

        def wait_stat(eng, index):
            if index % 2 == 0:
                eng.wait_ge(sq_used, C * (index // 2 + 1))
            else:
                eng.wait_ge(stat_done, (index + 1) // 2)

        def run_phase(eng, split, ph, even, odd):
            base, pairs, k = ph
            q0 = base // 2
            split(q0 + 1, 0, k)
            even(0)
            with eng.Fori(1, pairs - 1) as i:
                split(i + q0, 1, k)
                odd(i - 1)
                split(i + (q0 + 1), 0, k)
                even(i)
            i = pairs - 1
            split(q0 + i, 1, k)
            odd(i - 1)
            if base + 2 * pairs < UNITS:
                split(q0 + pairs, 0, blocks(base + 2 * pairs))
            even(i)
            odd(i)
            if base + 2 * pairs < UNITS:
                split(q0 + pairs, 1, blocks(base + 2 * pairs))

        def fixed(i):
            return isinstance(i, int)

        def page_number(eng, i, t):
            index = PAGES * i + t
            return eng.value_load(pages[0:1, bass.ds(index, 1)], min_val=0, max_val=N_PHYS - 1)

        def k_page_load(sp, i, t):
            if fixed(i) and t == 0:
                sp.wait_ge(s_pages, 16)
                sp.wait_ge(q_bd_zero, 1)
            if not fixed(i) or t >= 2:
                sp.wait_ge(k_used, PAGES * i + (t - 1))
            page = page_number(sp, i, t)
            sp.dma_start(k_page[t % 2][:], cache_kt[bass.ds(page, 1)].rearrange("a p h t -> (a p) h t"))\
                .then_inc(k_in[t % 2], 16)

        def z_cols(j):
            return ps[:].rearrange("p b c -> p (b c)")[:, 3 * j * 512:3 * j * 512 + KEY_COLS]

        def v_phase(split, v_half):
            q0 = VPROJ[0] // 2
            for n in range(2, 2 * VPROJ[1]):
                split(q0 + n // 2, n % 2, C)
                if n == 5:
                    v_half(0)
            split(QPROJ[0] // 2, 0, C)
            v_half(1)
            split(QPROJ[0] // 2, 1, C)

        @block.sync
        def _(sp):
            sp.dma_start(x[:], x_in).then_inc(s_x, 16)

            def ada_chunk(n, s, used):
                if used is not None:
                    sp.wait_ge(ada_done, used)
                sp.dma_start(ada_w[s][:], w_ada[bass.ds(n, 1)].rearrange("a p c -> (a p) c")).then_inc(ada_in[s], 16)

            def unit(q, s, src, row, n_cols):
                if not fixed(q) or q > 0:
                    sp.wait_ge(s_lo, 2 * q + (s - 1))
                sp.dma_start(raw[s][:, 0:n_cols], src[bass.ds(row, 1)].rearrange("a p c -> (a p) c"))\
                    .then_inc(w_in[s], 16)

            for n in range(ADA_FIRST):
                ada_chunk(n, n % ADA_RING, n - ADA_RING + 1 if n >= ADA_RING else None)
            for s in range(2):
                unit(0, s, w_k8, s, C * P)
            with sp.Fori(0, A_IN[1]) as i:
                for s in range(2):
                    unit(i + 1, s, w_k8, 2 * i + (s + 2), C * P)
                    for j in range(ADA_PER_UNIT):
                        n = ADA_FIRST + ADA_PER_UNIT * s + j
                        ada_chunk(2 * ADA_PER_UNIT * i + n, n % ADA_RING, 2 * ADA_PER_UNIT * i + (n - ADA_RING + 1))
            row = {C: 2 * A_IN[1], FH: 0}
            for ph in PHASES[1:]:
                base, pairs, k = ph
                skip = 1 if ph in (A_OUT, OPROJ) else 0
                src = w_k8 if k == C else w_down
                if ph == OPROJ:
                    for s in range(2):
                        unit(base // 2, s, src, row[k] + s, k * P)
                    for t in range(PAGES):
                        k_page_load(sp, 0, t)
                    with sp.Fori(1, NS) as i:
                        for t in range(PAGES):
                            k_page_load(sp, i, t)
                with sp.Fori(skip, pairs) as i:
                    for s in range(2):
                        unit(i + base // 2, s, src, 2 * i + (row[k] + s), k * P)
                row[k] += 2 * pairs
            for n in range(C):
                sp.wait_ge(x_ready, 3 * C + n + 1)
                sp.dma_start(y_out[:, n, :], x[:, n, :]).then_inc(x_stored, 16)
            sp.wait_ge(x_stored, 16 * C)

        @block.tensor
        def _(pe):
            flat = ps[:].rearrange("p b c -> p (b c)")

            def gemm_unit(q, s, k, hi, lo, tiles, ready=None):
                pe.wait_ge(s_lo, 2 * q + (s + 1))
                if not fixed(tiles) or tiles > 0:
                    pe.wait_ge(slot_free[s], tiles)
                for kb in range(k):
                    if ready is not None:
                        pe.wait_ge(ready[0], ready[1] + kb + 1)
                    for n, (w, v) in enumerate(((w_hi, hi), (w_hi, lo), (w_lo, hi))):
                        for b in range(2):
                            mm = pe.matmul(ps[:, 2 * s + b, 0:HALF], lhsT=w[s][:, kb * P:(kb + 1) * P],
                                           rhs=v[:, kb, b * HALF:(b + 1) * HALF],
                                           start=(kb == 0 and n == 0), stop=(kb == k - 1 and n == 2))
                mm.then_inc(gemm_done, 1)

            def phase(ph, hi, lo, ready):
                base, pairs, k = ph
                q0, t0 = base // 2, tiles_before(base)
                gemm_unit(q0, 0, k, hi, lo, t0, ready)
                gemm_unit(q0, 1, k, hi, lo, t0)
                with pe.Fori(1, pairs) as i:
                    for s in range(2):
                        gemm_unit(i + q0, s, k, hi, lo, i + t0)

            def ada_chunk(s, uses, out, first):
                pe.wait_ge(ada_in[s], uses)
                for kb in range(C):
                    mm = pe.matmul(out, lhsT=ada_w[s][:, kb * P:(kb + 1) * P], rhs=c_act[:, kb, :],
                                   start=(kb == 0), stop=(kb == C - 1), skip_group_check=True)
                mm.then_inc(ada_done, 1)

            def stat_matmuls(src, start, stop):
                for b in range(2):
                    mm = pe.matmul(ps[:, 2 * STAT + b, 0:HALF], lhsT=mean_w[:], rhs=src[:, b * HALF:(b + 1) * HALF],
                                   start=start, stop=stop)
                return mm

            def squares_sum(index):
                if index:
                    pe.wait_ge(rs_ready, index)
                for n in range(C):
                    pe.wait_ge(sq_ready, C * (index // 2) + n + 1)
                    stat_matmuls(sq[:, n % 2, :], n == 0, n == C - 1).then_inc(sq_used, 1)

            def y_sum_stat(index, r):
                pe.wait_ge(rs_ready, index)
                pe.wait_ge(y_acc, (C + 1) * (r + 1))
                stat_matmuls(y_sum[:], True, True).then_inc(stat_done, 1)

            pe.wait_ge(s_const, CONSTS)
            squares_sum(0)
            pe.wait_ge(c_ready, 1)
            for n in range(ADA_FIRST):
                ada_chunk(n % ADA_RING, 16 * (n // ADA_RING + 1), ps[:, 7, n * NB:(n + 1) * NB], n == 0)
            pe.wait_ge(mod_ready, 1)

            def a_in_pair(i, bank, first, ready=None):
                for s in range(2):
                    tiles = i if not fixed(i) or i > 0 else 0
                    gemm_unit(i, s, C, h_hi, h_lo, tiles, ready if s == 0 else None)
                    for j in range(ADA_PER_UNIT):
                        n = ADA_FIRST + ADA_PER_UNIT * s + j
                        col = (ADA_PER_UNIT * s + j) * NB + 2 * ADA_PER_UNIT * NB * (i - first)
                        ada_chunk(n % ADA_RING, 32 * i + 16 * (n // ADA_RING + 1), flat_cols(bank, col), False)

            def flat_cols(bank, col):
                return ps[:, bank, bass.ds(col, NB)]

            half = A_IN[1] // 2
            a_in_pair(0, 6, 0, (h_ready, 0))
            with pe.Fori(1, half) as i:
                a_in_pair(i, 6, 0)
            with pe.Fori(half, 2 * half) as i:
                a_in_pair(i, 7, half)

            pe.wait_ge(rs_ready, 1)
            for n in range(C):
                pe.wait_ge(taps, TAP_STEPS * (n + 1))
                pe.wait_ge(conv_seq, SEQ_STEPS * (n + 1))
                mm = stat_matmuls(y[:, n, :], n == 0, n == C - 1)
            mm.then_inc(stat_done, 1)
            squares_sum(2)
            phase(A_OUT, h_hi, h_lo, (h_ready, C))
            y_sum_stat(3, 0)
            squares_sum(4)

            def ffn(layer, norm, r, index):
                phase(UP[layer, 0], h_hi, h_lo, (h_ready, norm * C))
                phase(DOWN[layer, 0], act_hi, act_lo, (act_ready, 2 * layer * FH))
                phase(UP[layer, 1], h_hi, h_lo, None)
                phase(DOWN[layer, 1], act_hi, act_lo, (act_ready, (2 * layer + 1) * FH))
                y_sum_stat(index, r)

            ffn(0, 2, 1, 5)
            squares_sum(6)
            phase(KPROJ, h_hi, h_lo, (h_ready, 3 * C))
            pe.wait_ge(rs_ready, 7)
            for s in range(2):
                pe.wait_ge(slot_free[s], VPROJ[0] // 2)
            for n in range(2 * VPROJ[1]):
                s = n % 2
                pe.wait_ge(s_lo, VPROJ[0] + n + 1)
                if n == 4:
                    pe.wait_ge(v_act, 1)
                    pe.wait_ge(v_dve, 1)
                for j in range(2):
                    kb = 2 * (n % 4) + j
                    for t in range(5):
                        m = P if t < 4 else TT - 4 * P
                        for q, (a, w) in enumerate(((h_hi, w_hi), (h_lo, w_hi), (h_hi, w_lo))):
                            mm = pe.matmul(ps[0:m, t, :], lhsT=a[:, kb, t * P:t * P + m],
                                           rhs=w[s][:, j * 512:(j + 1) * 512],
                                           start=(kb == 0 and q == 0), stop=(kb == C - 1 and q == 2))
                mm.then_inc(gemm_done, 1)
            pe.wait_ge(v_act, 2)
            pe.wait_ge(v_dve, 2)
            phase(QPROJ, h_hi, h_lo, (h_ready, 4 * C))

            for s in range(2):
                pe.wait_ge(slot_free[s], tiles_before(OPROJ[0]))
            for j in range(2):
                r = slice(HD * j, HD * j + HD)
                for p in range(PAIRS):
                    mm = pe.matmul(ps[0:64, j, p * 64:(p + 1) * 64], lhsT=k_t[r, p, TP:TT], rhs=q_t[r, p, TP:TT],
                                   start=(p == 0), stop=True, skip_group_check=True)
            mm.then_inc(new_step, 1)
            pe.wait_ge(new_step, 1)
            for j in range(2):
                pe.matmul(ps[0:64, j, :], lhsT=one_row[0:1, 0:64],
                          rhs=bsb[0:1, j:HEADS:2].unsqueeze(2).to_broadcast([1, PAIRS, 64]),
                          start=False, stop=True, skip_group_check=True)
                mm = pe.matmul(ps[0:64, j, :], lhsT=ident[0:64, 0:64],
                               rhs=mask_new[0:64, :].unsqueeze(1).to_broadcast([64, PAIRS, 64]),
                               start=False, stop=True, skip_group_check=True)
            mm.then_inc(new_step, 1)
            pe.wait_ge(new_step, 6)
            for j in range(2):
                mm = pe.matmul(ps[0:64, j, :], lhsT=tri[0:64, 0:64], rhs=sp_new[:, j].rearrange("p a q -> p (a q)"),
                               start=False, stop=True, skip_group_check=True)
            mm.then_inc(new_step, 1)
            pe.wait_ge(new_step, 8)
            pe.wait_ge(mod_ready, 3)

            def chunk_cols(c):
                return ((0, 512), (512, 384), (1024, 256), (896, 128))[c]

            with pe.Fori(0, PAIRS) as i:
                def z_head(j):
                    r, b0 = HD * j, 3 * j * 512
                    for c in range(4):
                        at, n = chunk_cols(c)
                        pe.matmul(flat[:, b0 + at:b0 + at + n], lhsT=k_st[r:r + HD, c * P:(c + 1) * P],
                                  rhs=q_st[r:r + HD, c * P:TP], start=(c != 3), stop=True, skip_group_check=True)
                    for c in range(4):
                        at, n = chunk_cols(c)
                        mm = pe.matmul(flat[:, b0 + at:b0 + at + P], lhsT=ident[:], rhs=mask[:],
                                       start=False, stop=True, skip_group_check=True)
                    mm.then_inc(z_done, 1)

                def suffix_head(j):
                    pe.wait_ge(sp_done, 3 * i + (2 * j + 1))
                    b0 = 3 * j * 512
                    for c in range(4):
                        at, n = chunk_cols(c)
                        for c2 in range(c, 4):
                            at2, n2 = chunk_cols(c2)
                            mm = pe.matmul(flat[:, b0 + at + (c2 - c) * P:b0 + at + n],
                                           lhsT=(tri if c2 == c else neg_ones)[:], rhs=att[j][:, at2:at2 + n2],
                                           start=False, stop=True, skip_group_check=True)
                    mm.then_inc(suffixed, 1)

                def av_head(j):
                    pe.wait_ge(att_done, 3 * i + (2 * j + 1))
                    for c in range(4):
                        at, n = chunk_cols(c)
                        mm = pe.matmul(ps[HD * j:HD * j + HD, 6, c * P:TP], lhsT=v_st[:, c, HD * j:HD * j + HD],
                                       rhs=att[j][:, at:at + n], start=(c == 0), stop=(c == 3),
                                       skip_group_check=True)
                    mm.then_inc(av_done, 1)

                pe.wait_ge(kq_staged, 2 * i + 2)
                z_head(0)
                pe.wait_ge(seq_bank_free, i + 1)
                pe.wait_ge(pair_bank_free, i + 1)
                for c in range(4):
                    pe.wait_ge(k_in[c % 2], 32 * i + 16 * (c // 2 + 1))
                    for p in range(PAIRS):
                        mm = pe.matmul(ps[:, 7, c * P + p * 16:c * P + p * 16 + 16], lhsT=k_page[c % 2][:, p, :],
                                       rhs=q_bd[:, bass.ds(i, 1), p, :].rearrange("p a q -> p (a q)"),
                                       start=(c == 0 and p == 0), stop=True, skip_group_check=True)
                    mm.then_inc(k_used, 1)
                pe.matmul(ps[:, 7, :], lhsT=one_row[0:1, :],
                          rhs=bsb_seq[0:1, :].unsqueeze(1).to_broadcast([1, 4, P]),
                          start=False, stop=True, skip_group_check=True).then_inc(z_done, 1)
                z_head(1)
                suffix_head(0)
                pe.wait_ge(sp_done, 3 * i + 2)
                for c in range(4):
                    for c2 in range(c, 4):
                        pe.matmul(ps[:, 7, c * P:(c + 1) * P], lhsT=(tri if c2 == c else neg_ones)[:],
                                  rhs=att_s[:, c2 * P:(c2 + 1) * P], start=False, stop=True, skip_group_check=True)
                    mm = pe.matmul(ps[:, 7, c * P:(c + 1) * P], lhsT=neg_ones[0:64, :],
                                   rhs=sp_new[:, :, :, bass.ds(i * TS, TS)].rearrange("p j a q -> p a j q"),
                                   start=False, stop=True, skip_group_check=True)
                mm.then_inc(suffixed, 1)
                suffix_head(1)
                pe.wait_ge(v_staged, i + 1)
                av_head(0)
                pe.wait_ge(att_done, 3 * i + 2)
                for c in range(5):
                    if c < 4:
                        pe.wait_ge(v_in[c % 2], 32 * i + 16 * (c // 2 + 1))
                    for p in range(PAIRS):
                        if c < 4:
                            w, a = v_page[c % 2][:, p * P:(p + 1) * P], att_s[:, c * P + p * 16:c * P + p * 16 + 16]
                        else:
                            w = v_n[0:64, 4, p * P:(p + 1) * P]
                            a = att_new[:, :, p, bass.ds(i * TS, TS)]
                        mm = pe.matmul(ps[:, 7, p * 16:p * 16 + 16], lhsT=w, rhs=a,
                                       start=(c == 0 and p == 0), stop=(c == 4), skip_group_check=True)
                    mm.then_inc(v_used if c < 4 else av_done, 1)
                av_head(1)

            pe.wait_ge(seq_bank_free, NS + 1)
            pe.wait_ge(pair_bank_free, PAIRS + 1)
            phase(OPROJ, h_hi, h_lo, None)
            y_sum_stat(7, 2)
            squares_sum(8)
            ffn(1, 5, 3, 9)

        @block.scalar
        def _(act):
            act.dma_start(c_raw[:], c_in).then_inc(s_c, 16)
            act.dma_start(par[:], par_in).then_inc(s_par, 16)
            act.wait_ge(s_c, 16)
            act.activation(c_act[:], c_raw[:], ACT.Silu).then_inc(c_ready, 1)

            def split(q, s, k):
                act.wait_ge(w_in[s], 16 * q + 16)
                if not fixed(q) or q > 0:
                    act.wait_ge(gemm_done, 2 * q + (s - 1))
                act.activation(w_hi[s][:, 0:k * P], raw[s][:, 0:k * P], ACT.Copy).then_inc(s_hi, 1)

            def rms(index):
                wait_stat(act, index)
                act.activation(two(rs[:]), slot(STAT), ACT.Ln, bias=eps_col[:, 0:1]).then_inc(ln_step, 1)
                act.wait_ge(ln_step, max(index, 1))
                act.activation(rs[:], rs[:], ACT.Exp, scale=-0.5).then_inc(rs_ready, 1)

            def squares(norm, src, ready, first):
                for n in range(C):
                    if ready is not None:
                        act.wait_ge(ready, first + n + 1)
                    if n >= 2:
                        act.wait_ge(sq_used, norm * C + n - 1)
                    act.activation(sq[:, n % 2, :], src[:, n, :], ACT.Square).then_inc(sq_ready, 1)

            def modulate(norm, shift=None, at=0):
                for n in range(C):
                    act.wait_ge(hn_x, norm * C + n + 1)
                    if shift is None:
                        act.activation(hn[:, n % 2, :], hn[:, n % 2, :], ACT.Silu, bias=prm("ln_a_b", n),
                                       scale=prm("ln_a_g", n)).then_inc(hn_p, 1)
                    else:
                        act.activation(hn[:, n % 2, 0:TP], hn[:, n % 2, 0:TP], ACT.Identity,
                                       bias=shift[:, at + n, 0:1], scale=a_mod[:, n, 0:1]).then_inc(hn_p, 1)

            act.wait_ge(s_const, CONSTS)
            act.wait_ge(s_par, 16)
            act.wait_ge(s_x, 16)
            squares(0, x, None, 0)
            rms(0)
            split(0, 0, C)
            split(0, 1, C)
            modulate(0, mod[:, 0], 0)

            def gate_a(i):
                act.wait_ge(gemm_done, 2 * i + 1)
                if not fixed(i) or i > 0:
                    act.wait_ge(slot_free[1], i)
                act.activation(two(sig[:]), slot(0), ACT.Sigmoid).then_inc(slot_free[0], 1)

            run_phase(act, split, A_IN, gate_a, lambda i: None)

            wait_stat(act, 1)
            act.activation(two(mu[:]), slot(STAT), ACT.Copy).then_inc(rs_ready, 1)
            squares(1, y, conv_centred, 0)
            rms(2)
            modulate(1)

            def finish(r, ph, copy):
                def handler(i, s):
                    m = 2 * i + s
                    if copy:
                        act.wait_ge(gemm_done, m + (ph[0] + 1))
                    else:
                        act.wait_ge(slot_free[s], i + (tiles_before(ph[0]) + 1))
                    if not fixed(m) or m >= 2:
                        act.wait_ge(y_acc, 2 * i + (s + r * (C + 1)))
                    if copy:
                        act.activation(two(sq[:, s, :]), slot(s), ACT.Square).then_inc(y_sq, 1)
                        act.activation(two(chunk(y, 2 * i + s)), slot(s), ACT.Copy).then_inc(slot_free[s], 1)
                        act.wait_ge(slot_free[s], i + (tiles_before(ph[0]) + 1))
                    else:
                        act.activation(sq[:, s, :], chunk(y, 2 * i + s), ACT.Square).then_inc(y_sq, 1)
                        act.wait_ge(y_sq, m + (r * C + 1))
                    act.activation(chunk(y, m, 0, TP), chunk(y, m, 0, TP), ACT.Copy, scale=chunk(g_mod, m, 0, 1))\
                        .then_inc(y_scaled, 1)
                return (lambda i: handler(i, 0)), (lambda i: handler(i, 1))

            act.wait_ge(coef_ready, 2)
            run_phase(act, split, A_OUT, *finish(0, A_OUT, True))
            rms(3)
            squares(2, x, x_ready, 0)
            rms(4)
            modulate(2, mod[:, 0], 3 * C)

            def ffn(layer, r):
                for hf in range(2):
                    ph = UP[layer, hf]
                    g0 = (2 * layer + hf) * FH
                    f0 = layer * FC + hf * FH

                    def gate_f(i):
                        g = i + g0
                        act.wait_ge(gemm_done, 2 * i + (ph[0] + 1))
                        if not fixed(g) or g > 0:
                            act.wait_ge(conv_done, g)
                            act.wait_ge(tail_saved, 2 * g)
                            act.wait_ge(gelu_done, g)
                        act.activation(g_pad[:, 2:2 + HALF], ps[:, 0, 0:HALF], ACT.Copy).then_inc(gate_copied, 1)
                        act.activation(g_pad[:, 2 + HALF:2 + TP], ps[:, 1, 0:TP - HALF], ACT.Copy)\
                            .then_inc(gate_copied, 1)
                        act.activation(g_seq[:, :, 2:2 + TS], seq(ps[:, 1, TP - HALF:HALF]), ACT.Copy)\
                            .then_inc(gate_copied, 1)
                        act.wait_ge(gate_copied, 3 * g + 3)
                        w, b = prm("w_ffn_dw", (i + f0) * WF + 2), prm("b_ffn_dw", i + f0)
                        act.activation(cv[:, 0:TP], g_pad[:, 2:2 + TP], ACT.Identity, bias=b, scale=w)\
                            .then_inc(slot_free[0], 1)
                        act.activation(seq(cv[:, TP:TT]), g_seq[:, :, 2:2 + TS], ACT.Identity, bias=b, scale=w)\
                            .then_inc(cv_tap, 1)

                    def value_f(i):
                        g = i + g0
                        act.wait_ge(gemm_done, 2 * i + (ph[0] + 2))
                        if not fixed(g) or g > 0:
                            act.wait_ge(prod_done, g)
                        act.activation(two(val[:]), slot(1), ACT.Copy).then_inc(slot_free[1], 1)
                        act.wait_ge(conv_done, g + 1)
                        act.activation(ge[:], cv[:], ACT.Gelu_apprx_tanh).then_inc(gelu_done, 1)

                    run_phase(act, split, ph, gate_f, value_f)
                    down = DOWN[layer, hf]
                    if hf == 0:
                        def part(i, s):
                            act.wait_ge(gemm_done, 2 * i + (down[0] + s + 1))
                            act.activation(two(chunk(y, 2 * i + s)), slot(s), ACT.Copy).then_inc(slot_free[s], 1)
                        run_phase(act, split, down, lambda i: part(i, 0), lambda i: part(i, 1))
                    else:
                        run_phase(act, split, down, *finish(r, down, False))

            ffn(0, 1)
            rms(5)
            squares(3, x, x_ready, C)
            rms(6)
            modulate(3, no_shift, 0)

            def projected(ph, dst, scale):
                def handler(i, s):
                    act.wait_ge(gemm_done, 2 * i + (ph[0] + s + 1))
                    act.activation(two(chunk(dst, 2 * i + s)), slot(s), ACT.Copy, scale=scale)\
                        .then_inc(slot_free[s], 1)
                return (lambda i: handler(i, 0)), (lambda i: handler(i, 1))

            run_phase(act, split, KPROJ, *projected(KPROJ, k_t, 1.0))

            def v_half(hf):
                act.wait_ge(gemm_done, VPROJ[0] + 4 * hf + 4)
                for t in (0, 2, 4):
                    m = P if t < 4 else TT - 4 * P
                    a = act.activation(v_n[0:m, t, hf * 512:(hf + 1) * 512], ps[0:m, t, :], ACT.Copy)
                a.then_inc(v_act, 1)

            v_phase(split, v_half)
            modulate(4, mod[:, 1], 0)
            run_phase(act, split, QPROJ, *projected(QPROJ, q_t, HD ** -0.5))

            act.wait_ge(new_step, 3)
            act.activation(sp_new[:], sp_new[:], ACT.Exp).then_inc(new_step, 1)
            act.wait_ge(new_step, 4)
            act.activation(sp_new[:], sp_new[:], ACT.Ln, bias=1.0).then_inc(new_step, 1)
            act.wait_ge(new_step, 7)
            act.activation(att_new[:].rearrange("p j a q -> p j (a q)"), ps[0:64, 0:2, :], ACT.Exp)\
                .then_inc(new_step, 1)

            def stage(i):
                act.activation(k_st[:, 0:TP], chunk(k_t, i, 0, TP), ACT.Copy).then_inc(kq_staged, 1)
                act.activation(q_st[:, 0:TP], chunk(q_t, i, 0, TP), ACT.Copy).then_inc(kq_staged, 1)

            def attend(i, last):
                order = (att[0][:], att_s[:], att[1][:])
                for n, tile in enumerate(order):
                    act.wait_ge(clamped, 3 * i + (n + 1))
                    act.activation(tile, tile, ACT.Exp).then_inc(exped, 1)
                    act.wait_ge(exped, 3 * i + (n + 1))
                    act.activation(tile, tile, ACT.Ln, bias=1.0).then_inc(lned, 1)
                if not last:
                    act.wait_ge(z_done, 3 * i + 3)
                    stage(i + 1)
                for n, tile in enumerate(order):
                    act.wait_ge(suffixed, 3 * i + (n + 1))
                    if n == 1:
                        act.activation(tile, ps[:, 7, :], ACT.Exp).then_inc(att_done, 1)
                    else:
                        act.activation(tile, z_cols(n // 2), ACT.Exp, bias=bsb[:, bass.ds(2 * i + n // 2, 1)])\
                            .then_inc(att_done, 1)

            stage(0)
            with act.Fori(0, PAIRS - 1) as i:
                attend(i, False)
            attend(PAIRS - 1, True)

            act.wait_ge(coef_ready, 7)
            run_phase(act, split, OPROJ, *finish(2, OPROJ, True))
            rms(7)
            squares(4, x, x_ready, 2 * C)
            rms(8)
            modulate(5, mod[:, 1], 3 * C)
            ffn(1, 3)
            rms(9)

        @block.vector
        def _(dve):
            def split(q, s, k):
                dve.wait_ge(s_hi, 2 * q + (s + 1))
                dve.tensor_tensor(w_lo[s][:, 0:k * P], raw[s][:, 0:k * P], w_hi[s][:, 0:k * P].bitcast(F32),
                                  ALU.subtract).then_inc(s_lo, 1)

            def scale_coef(l, at, gain):
                dve.scalar_tensor_tensor(out=a_mod[:], in0=mod[:, l, at:at + C, :], scalar=1.0, in1=gain_of(gain, l),
                                         op0=ALU.add, op1=ALU.mult).then_inc(coef_ready, 1)

            def gate_coef(l, at, gain):
                dve.tensor_tensor(g_mod[:], mod[:, l, at:at + C, :], gain_of(gain, l), ALU.mult)\
                    .then_inc(coef_ready, 1)

            def gain_of(name, l):
                return par[:, PAR[name] + l * C:PAR[name] + (l + 1) * C].unsqueeze(2).to_broadcast([P, C, NB])

            def bias_mod(first, count, bank):
                b = par[:, PAR["b_ada"] + first:PAR["b_ada"] + first + count].unsqueeze(2).to_broadcast([P, count, NB])
                out = mod[:].rearrange("p l c b -> p (l c) b")[:, first:first + count, :]
                src = ps[:, bank, 0:count * NB].rearrange("p (c b) -> p c b", b=NB)
                dve.tensor_tensor(out, src, b, ALU.add).then_inc(mod_ready, 1)

            def apply_norm(norm, src, index, multiplied, seq_norm):
                dve.wait_ge(rs_ready, index + 1)
                if multiplied:
                    dve.wait_ge(gemm_done, multiplied)

                def finish(n):
                    g = norm * C + n
                    dve.wait_ge(hn_p, g + 1)
                    if seq_norm is not None:
                        dve.wait_ge(hn_s, 2 * (seq_norm * C + n + 1))
                    dve.tensor_copy(h_hi[:, n, :], hn[:, n % 2, :]).then_inc(h_hi_ready, 1)
                    dve.wait_ge(h_hi_ready, g + 1)
                    dve.tensor_tensor(h_lo[:, n, :], hn[:, n % 2, :], h_hi[:, n, :].bitcast(F32), ALU.subtract)\
                        .then_inc(h_ready, 1)

                for n in range(C):
                    if n >= 2:
                        dve.wait_ge(h_ready, norm * C + n - 1)
                    dve.tensor_tensor(hn[:, n % 2, :], src[:, n, :], rs[:], ALU.mult).then_inc(hn_x, 1)
                    if n:
                        finish(n - 1)
                finish(C - 1)

            def residual(r, index):
                dve.wait_ge(rs_ready, index + 1)

                def add(n):
                    dve.wait_ge(y_normed, r * C + n + 1)
                    dve.tensor_tensor(x[:, n, :], x[:, n, :], y[:, n, :], ALU.add).then_inc(x_ready, 1)

                for n in range(C):
                    dve.wait_ge(y_scaled, r * C + n + 1)
                    dve.wait_ge(y_scaled_s, r * C + n + 1)
                    dve.tensor_tensor(y[:, n, :], y[:, n, :], rs[:], ALU.mult).then_inc(y_normed, 1)
                    if n:
                        add(n - 1)
                add(C - 1)

            dve.wait_ge(s_par, 16)
            split(0, 0, C)
            split(0, 1, C)
            dve.wait_ge(ada_done, ADA_FIRST)
            bias_mod(0, ADA_FIRST, 7)
            dve.wait_ge(mod_ready, 1)
            scale_coef(0, C, "g_pre_mix")
            apply_norm(0, x, 0, 0, 0)

            def tap(i, k):
                g = TAP_STEPS * i
                if k:
                    dve.wait_ge(taps, g + (k - 1))
                elif not fixed(i) or i > 0:
                    dve.wait_ge(taps, g)
                out = odd_taps[:] if k % 2 else chunk(y, i, 0, TP)
                src = chunk(u_p, i, k, k + TP) if k < WA else None
                if k == WA:
                    out = chunk(y, i, 0, TP)
                    dve.wait_ge(taps, g + k)
                    ins = dve.tensor_tensor(out, out, odd_taps[:], ALU.add)
                elif k == 0:
                    ins = dve.tensor_scalar(out, src, prm("w_a_dw", i * WA), prm("b_a_dw", i), ALU.mult, ALU.add)
                elif k == 1:
                    ins = dve.tensor_scalar(out, src, prm("w_a_dw", i * WA + k), None, ALU.mult)
                else:
                    ins = dve.scalar_tensor_tensor(out=out, in0=src, scalar=prm("w_a_dw", i * WA + k), in1=out,
                                                   op0=ALU.mult, op1=ALU.add)
                ins.then_inc(taps, 1)

            def glu(i):
                dve.wait_ge(slot_free[0], i + 1)
                dve.wait_ge(gemm_done, 2 * i + 2)
                parts = ((chunk(u_p, i, WA - 1, WA - 1 + HALF), ps[:, 2, 0:HALF], sig[:, 0:HALF]),
                         (chunk(u_p, i, WA - 1 + HALF, WA - 1 + TP), ps[:, 3, 0:TP - HALF], sig[:, HALF:TP]),
                         (u_s[:, bass.ds(i, 1), :, WA - 1:WA - 1 + TS].rearrange("p a s t -> p (a s) t"),
                          seq(ps[:, 3, TP - HALF:HALF]), seq(sig[:, TP:TT])))
                for out, a, b in parts:
                    ins = dve.tensor_tensor(out, a, b, ALU.mult)
                ins.then_inc(slot_free[1], 1)
                dve.wait_ge(slot_free[1], i + 1)
                for k in range(WA // 2):
                    tap(i, k)

            def later_taps(i):
                if fixed(i) and i == 0:
                    return
                for k in range(WA // 2, WA + 1):
                    tap(i - 1, k)

            dve.wait_ge(pads_ready, 1)
            run_phase(dve, split, A_IN, later_taps, glu)
            later_taps(A_IN[1])
            dve.wait_ge(ada_done, 2 * MODS)
            bias_mod(ADA_FIRST, ADA_PER_UNIT * A_IN[1], 6)
            bias_mod(ADA_FIRST + ADA_PER_UNIT * A_IN[1], ADA_PER_UNIT * A_IN[1], 7)
            dve.wait_ge(mod_ready, 3)
            gate_coef(0, 2 * C, "g_post_mix")
            dve.wait_ge(rs_ready, 2)
            for n in range(C):
                dve.tensor_tensor(y[:, n, :], y[:, n, :], mu[:], ALU.subtract).then_inc(conv_centred, 1)
            apply_norm(1, y, 2, 2 * A_IN[1], None)
            dve.wait_ge(conv_stored, 32)

            def y_squares(r, ph, add):
                def handler(i, s):
                    if add:
                        dve.wait_ge(gemm_done, 2 * i + (ph[0] + s + 1))
                        yc = two(chunk(y, 2 * i + s))
                        dve.tensor_tensor(yc, slot(s), yc, ALU.add).then_inc(slot_free[s], 1)
                    if s == 1:
                        acc(2 * i, 0)
                    elif not fixed(i) or i > 0:
                        acc(2 * i - 1, 1)

                def acc(m, s):
                    dve.wait_ge(y_sq, m + (r * C + 1))
                    dve.wait_ge(y_acc, m + (r * (C + 1) + 1))
                    dve.tensor_tensor(y_sum[:], y_sum[:], sq[:, s, :], ALU.add).then_inc(y_acc, 1)

                dve.memset(y_sum[:], 0.0).then_inc(y_acc, 1)
                run_phase(dve, split, ph, lambda i: handler(i, 0), lambda i: handler(i, 1))
                acc(C - 1, 1)

            y_squares(0, A_OUT, False)
            scale_coef(0, 4 * C, "g_pre_ffn")
            residual(0, 3)
            apply_norm(2, x, 4, A_OUT[0] + 2 * A_OUT[1], 1)

            def ffn(layer, r):
                gate_coef(layer, 5 * C, "g_post_ffn")
                for hf in range(2):
                    ph = UP[layer, hf]
                    g0 = (2 * layer + hf) * FH
                    f0 = layer * FC + hf * FH

                    def conv(i):
                        g = i + g0
                        dve.wait_ge(cv_tap, g + 1)
                        dve.wait_ge(state_put, g + 1)
                        for j in (1, 0):
                            w = prm("w_ffn_dw", (i + f0) * WF + j)
                            if j == 0:
                                dve.wait_ge(conv_step, 3 * g + 2)
                            dve.scalar_tensor_tensor(out=cv[:, 0:TP], in0=g_pad[:, j:j + TP], scalar=w,
                                                     in1=cv[:, 0:TP], op0=ALU.mult, op1=ALU.add).then_inc(conv_step, 1)
                            last = dve.scalar_tensor_tensor(out=seq(cv[:, TP:TT]), in0=g_seq[:, :, j:j + TS],
                                                            scalar=w, in1=seq(cv[:, TP:TT]), op0=ALU.mult,
                                                            op1=ALU.add)
                            last.then_inc(conv_step if j else conv_done, 1)

                    def gated(i):
                        g = i + g0
                        dve.wait_ge(gelu_done, g + 1)
                        if not fixed(g) or g > 0:
                            dve.wait_ge(act_ready, g)
                        dve.tensor_tensor(prod[:], ge[:], val[:], ALU.mult).then_inc(prod_done, 1)
                        dve.wait_ge(prod_done, g + 1)
                        dve.tensor_copy(chunk(act_hi, i), prod[:]).then_inc(act_hi_done, 1)
                        dve.wait_ge(act_hi_done, g + 1)
                        dve.tensor_tensor(chunk(act_lo, i), prod[:], chunk(act_hi, i).bitcast(F32), ALU.subtract)\
                            .then_inc(act_ready, 1)

                    run_phase(dve, split, ph, conv, gated)
                    if hf == 0:
                        run_phase(dve, split, DOWN[layer, 0], lambda i: None, lambda i: None)
                    else:
                        y_squares(r, DOWN[layer, 1], True)

            ffn(0, 1)
            dve.tensor_copy(a_mod[:], par[:, PAR["g_kv"]:PAR["g_kv"] + C].unsqueeze(2).to_broadcast([P, C, NB]))\
                .then_inc(coef_ready, 1)
            residual(1, 5)
            apply_norm(3, x, 6, DOWN[0, 1][0] + 8, 2)
            run_phase(dve, split, KPROJ, lambda i: None, lambda i: None)

            def v_half(hf):
                dve.wait_ge(gemm_done, VPROJ[0] + 4 * hf + 4)
                for t in (1, 3):
                    ins = dve.tensor_copy(v_n[:, t, hf * 512:(hf + 1) * 512], ps[:, t, :])
                ins.then_inc(v_dve, 1)

            v_phase(split, v_half)
            scale_coef(1, C, "g_pre_mix")
            apply_norm(4, x, 6, VPROJ[0] + 8, 3)
            gate_coef(1, 2 * C, "g_post_mix")
            run_phase(dve, split, QPROJ, lambda i: None, lambda i: None)

            dve.wait_ge(q_bd_zero, 1)
            for s in range(2):
                dve.wait_ge(slot_free[s], tiles_before(OPROJ[0]))
            for j, free in enumerate((seq_bank_free, pair_bank_free)):
                r = slice(HD * j, HD * j + HD)
                dve.tensor_copy(q_bd[r, :, :, TS * j:TS * j + TS],
                                q_t[r, :, TP:TT].rearrange("p a (s q) -> p s a q", s=NS)).then_inc(free, 1)
            new_ps = ps[0:64, 0:2, :]
            new_sp = sp_new[:].rearrange("p j a q -> p j (a q)")
            dve.wait_ge(new_step, 2)
            dve.tensor_scalar(new_sp, new_ps, SP_CLAMP, None, ALU.min).then_inc(new_step, 1)
            dve.wait_ge(new_step, 5)
            dve.tensor_tensor(new_sp, new_ps, new_sp, ALU.max).then_inc(new_step, 1)

            with dve.Fori(0, PAIRS) as i:
                def clamp(n):
                    dve.wait_ge(z_done, 3 * i + (n + 1))
                    if n == 1:
                        ins = dve.tensor_scalar(att_s[:], ps[:, 7, :], SP_CLAMP, None, ALU.min)
                    else:
                        ins = dve.tensor_scalar(att[n // 2][:], z_cols(n // 2), bsb[:, bass.ds(2 * i + n // 2, 1)],
                                                SP_CLAMP, ALU.add, ALU.min)
                    ins.then_inc(clamped, 1)

                def softplus(n):
                    dve.wait_ge(lned, 3 * i + (n + 1))
                    if n == 1:
                        ins = dve.tensor_tensor(att_s[:], ps[:, 7, :], att_s[:], ALU.max)
                    else:
                        a = att[n // 2][:]
                        ins = dve.scalar_tensor_tensor(out=a, in0=z_cols(n // 2), scalar=bsb[:, bass.ds(2 * i + n // 2, 1)],
                                                       in1=a, op0=ALU.add, op1=ALU.max)
                    ins.then_inc(sp_done, 1)

                clamp(0)
                clamp(1)
                softplus(0)
                clamp(2)
                softplus(1)
                softplus(2)
                dve.wait_ge(av_done, 3 * i + 2)
                for lo in range(2):
                    for j in range(2):
                        r = slice(HD * j, HD * j + HD)
                        src = ps[r, 7, 0:P].rearrange("p (a b) -> p a b", b=2 * TS)[:, :, TS * j:TS * j + TS]
                        hi = h_hi[r, :, bass.ds(i * TS + TP, TS)]
                        if lo:
                            if j == 0:
                                dve.wait_ge(o_hi_done, 2 * i + 1)
                            ins = dve.tensor_tensor(h_lo[r, :, bass.ds(i * TS + TP, TS)], src, hi.bitcast(F32), ALU.subtract)
                        else:
                            ins = dve.tensor_copy(hi, src)
                    ins.then_inc(seq_bank_free if lo else o_hi_done, 1)
                dve.wait_ge(av_done, 3 * i + 3)
                dve.tensor_copy(chunk(h_hi, i, 0, TP), ps[:, 6, :]).then_inc(o_hi_done, 1)
                dve.wait_ge(o_hi_done, 2 * i + 2)
                dve.tensor_tensor(chunk(h_lo, i, 0, TP), ps[:, 6, :], chunk(h_hi, i, 0, TP).bitcast(F32), ALU.subtract)\
                    .then_inc(pair_bank_free, 1)

            y_squares(2, OPROJ, False)
            scale_coef(1, 4 * C, "g_pre_ffn")
            residual(2, 7)
            apply_norm(5, x, 8, OPROJ[0] + 8, 4)
            ffn(1, 3)
            residual(3, 9)

        @block.gpsimd
        def _(pool):
            pool.dma_start(bsb[:], b_sb_in.partition_broadcast(P)).then_inc(s_bsb, 16)
            pool.dma_start(pages[:], page_table).then_inc(s_pages, 16)
            pool.dma_start(u_s[:, :, :, 0:WA - 1].rearrange("p c s t -> p (c s) t"), state_a).then_inc(s_state, 16)
            pool.memset(eps_col[:], EPS).then_inc(s_const, 1)
            pool.memset(no_shift[:], 0.0).then_inc(s_const, 1)
            pool.memset(mean_w[:], 1.0 / D).then_inc(s_const, 1)
            pool.memset(one_row[:], 1.0).then_inc(s_const, 1)
            pool.memset(neg_ones[:], -1.0).then_inc(s_const, 1)
            pool.memset(ident[:], 1.0).then_inc(s_const, 1)
            pool.memset(mask[:], -1e30).then_inc(s_const, 1)
            pool.memset(mask_new[:], 0.0).then_inc(s_const, 1)
            pool.memset(tri[:], -1.0).then_inc(s_const, 1)
            pool.memset(u_p[:, :, 0:WA - 1], 0.0).then_inc(pads_ready, 1)
            pool.wait_ge(s_const, 9)
            pool.affine_select(out=tri[:], in_=tri[:], compare_op=ALU.is_ge, fill=0.0, base=0, pattern=[[-1, P]],
                               channel_multiplier=1).then_inc(s_const, 1)
            pool.affine_select(out=ident[:], in_=ident[:], compare_op=ALU.is_equal, fill=0.0, base=0,
                               pattern=[[-1, P]], channel_multiplier=1).then_inc(s_const, 1)
            pool.affine_select(out=mask[:], in_=mask[:], compare_op=ALU.is_ge, fill=0.0, base=0, pattern=[[-1, P]],
                               channel_multiplier=1).then_inc(s_const, 1)
            m3 = mask_new[:].rearrange("p (s q) -> p s q", s=NS)
            for n, (base, cm, pattern) in enumerate(((-1, -1, [[TS, NS], [1, TS]]), (0, 1, [[-TS, NS], [0, TS]]),
                                                     (TS - 1, -1, [[TS, NS], [0, TS]]))):
                pool.wait_ge(s_const, 12 + n)
                pool.affine_select(out=m3, in_=m3, compare_op=ALU.is_ge, fill=-1e30, base=base, pattern=pattern,
                                   channel_multiplier=cm).then_inc(s_const, 1)
            pool.wait_ge(s_bsb, 16)
            pool.wait_ge(s_const, 15)
            pool.tensor_copy(bsb_seq[:].rearrange("p (h q) -> p h q", q=TS),
                             bsb[:].unsqueeze(2).to_broadcast([P, HEADS, TS])).then_inc(s_const, 1)

            def modulate_seq(norm, shift, at):
                k = {0: 0, 2: 1, 3: 2, 4: 3, 5: 4}[norm]
                for n in range(C):
                    t = seq(hn[:, n % 2, TP:TT])
                    pool.wait_ge(hn_x, norm * C + n + 1)
                    pool.tensor_tensor(t, t, per_seq(a_mod, n), ALU.mult).then_inc(hn_s, 1)
                    pool.wait_ge(hn_s, 2 * (k * C + n) + 1)
                    pool.tensor_tensor(t, t, shift[:, at + n, 1:NB].unsqueeze(2).to_broadcast([P, NS, TS]), ALU.add)\
                        .then_inc(hn_s, 1)

            modulate_seq(0, mod[:, 0], 0)

            pool.wait_ge(s_state, 16)
            with pool.Fori(0, C) as i:
                def bcast(col):
                    return w_seq[:, col:col + 1].unsqueeze(2).to_broadcast([P, NS, TS])

                def product(k, dst):
                    pool.tensor_tensor(dst, u_seq[:, :, k:k + TS], bcast(k), ALU.mult).then_inc(conv_seq, 1)

                def add(term):
                    pool.tensor_tensor(y_seq[:], y_seq[:], term, ALU.add).then_inc(conv_seq, 1)

                g = SEQ_STEPS * i
                pool.wait_ge(slot_free[1], i + 1)
                pool.tensor_copy(u_seq[:], u_s[:, bass.ds(i, 1), :, :].rearrange("p a s t -> p (a s) t"))\
                    .then_inc(conv_seq, 1)
                pool.tensor_copy(w_seq[:, 0:WA], prm("w_a_dw", i * WA, WA)).then_inc(conv_seq, 1)
                pool.tensor_copy(w_seq[:, WA:WA + 1], prm("b_a_dw", i)).then_inc(conv_seq, 1)
                pool.wait_ge(conv_seq, g + 3)
                product(0, y_seq[:])
                product(1, s_prod[:, 1])
                pool.wait_ge(conv_seq, g + 4)
                add(bcast(WA))
                for k in range(2, WA):
                    pool.wait_ge(conv_seq, g + (2 * k + 2))
                    product(k, s_prod[:, k % 2])
                    add(s_prod[:, (k - 1) % 2])
                pool.wait_ge(conv_seq, g + (2 * WA + 2))
                add(s_prod[:, (WA - 1) % 2])
                pool.wait_ge(conv_seq, g + (2 * WA + 3))
                pool.tensor_copy(seq(chunk(y, i, TP, TT)), y_seq[:]).then_inc(conv_seq, 1)
            pool.dma_start(conv_a_p, u_p[:, :, TP:TP + WA - 1]).then_inc(conv_stored, 16)
            pool.dma_start(conv_a_s, u_s[:, :, :, TS:TS + WA - 1].rearrange("p c s t -> p (c s) t")).then_inc(conv_stored, 16)

            def scale_seq(r, coef):
                pool.wait_ge(coef_ready, coef)
                with pool.Fori(0, C) as i:
                    pool.wait_ge(y_scaled, i + (r * C + 1))
                    t = seq(chunk(y, i, TP, TT))
                    pool.tensor_tensor(t, t, chunk(g_mod, i, 1, NB).unsqueeze(2).to_broadcast([P, NS, TS]), ALU.mult)\
                        .then_inc(y_scaled_s, 1)

            def ffn(layer, r, coef):
                pool.dma_start(f_state[:], state_f[layer]).then_inc(s_fstate, 16)
                pool.memset(g_pad[:, 0:WF - 1], 0.0).then_inc(pads_ready, 1)
                pool.wait_ge(s_fstate, 16 * (layer + 1))
                g0 = layer * FC

                def save_tail(i):
                    g = i + g0
                    pool.wait_ge(gate_copied, 3 * g + 3)
                    t = tails[:, bass.ds(i, 1), :].rearrange("p a t -> p (a t)")
                    pool.tensor_copy(t[:, 0:2], g_pad[:, TP:TP + 2]).then_inc(tail_saved, 1)
                    pool.tensor_copy(t[:, 2:].rearrange("p (s t) -> p s t", t=2), g_seq[:, :, TS:TS + 2])\
                        .then_inc(tail_saved, 1)

                def put_state(i):
                    pool.tensor_copy(g_seq[:, :, 0:2], f_state[:, bass.ds(i, 1), :]
                                     .rearrange("p a (s t) -> p (a s) t", t=2)).then_inc(state_put, 1)

                put_state(0)
                save_tail(0)
                with pool.Fori(1, FC) as i:
                    pool.wait_ge(conv_done, i + g0)
                    put_state(i)
                    save_tail(i)
                pool.wait_ge(tail_saved, 2 * (g0 + FC))
                pool.dma_start(ffn_tails[layer], tails[:]).then_inc(tails_stored, 16)
                scale_seq(r, coef)

            scale_seq(0, 2)
            modulate_seq(2, mod[:, 0], 3 * C)
            ffn(0, 1, 4)
            modulate_seq(3, no_shift, 0)
            for s in range(2):
                pool.wait_ge(slot_free[s], VPROJ[0] // 2)
            pool.dma_start(k_out, k_t[:]).then_inc(kv_stored, 16)
            pool.wait_ge(v_act, 2)
            pool.wait_ge(v_dve, 2)
            pool.dma_start(v_out[0:TP].rearrange("(t p) c -> p t c", p=P), v_n[:, 0:4, :]).then_inc(kv_stored, 16)
            pool.dma_start(v_out[TP:TT], v_n[0:TT - TP, 4, :]).then_inc(kv_stored, 16)
            modulate_seq(4, mod[:, 1], 0)
            pool.wait_ge(h_ready, 5 * C)
            pool.wait_ge(tails_stored, 16)
            pool.memset(q_bd[:], 0.0).then_inc(q_bd_zero, 1)

            def v_page_load(i, t):
                if not fixed(i) or t >= 2:
                    pool.wait_ge(v_used, PAGES * i + (t - 1))
                page = page_number(pool, i, t)
                pool.dma_start(v_page[t % 2][:], cache_v[bass.ds(page, 1)].rearrange("a p c -> (a p) c"))\
                    .then_inc(v_in[t % 2], 16)

            def stage_v(i):
                pool.tensor_copy(v_st[:, 0:4, :], v_n[:, 0:4, bass.ds(i * P, P)]).then_inc(v_staged, 1)

            pool.wait_ge(s_pages, 16)
            stage_v(0)
            for t in range(PAGES):
                v_page_load(0, t)
            with pool.Fori(1, NS) as i:
                for t in range(2):
                    v_page_load(i, t)
                pool.wait_ge(av_done, 3 * i)
                stage_v(i)
                for t in range(2, PAGES):
                    v_page_load(i, t)
            scale_seq(2, 7)
            modulate_seq(5, mod[:, 1], 3 * C)
            ffn(1, 3, 9)
            pool.wait_ge(conv_stored, 32)
            pool.wait_ge(kv_stored, 48)
            pool.wait_ge(tails_stored, 32)


_OUTS = [("y_t", (P, C, TT)), ("conv_a_p", (P, C, WA - 1)), ("conv_a_s", (P, C * NS, WA - 1)),
         ("ffn_tails", (DEPTH, P, FC, 2 * NB)), ("k_t", (P, PAIRS, TT)), ("v", (TT, D))]


def _blocks(w, k, cols):
    return w.reshape(k, P, -1, cols).transpose(2, 1, 0, 3).reshape(-1, P, k * cols)


def _features(a):
    a = a.reshape(*a.shape[:-1], -1, P)
    return np.moveaxis(a, -1, 0)


def kernel(**inputs):
    import concourse.bacc as bacc
    from concourse.bass_utils import run_bass_kernel_spmd

    v = {name: np.asarray(a) for name, a in inputs.items()}
    tokens = np.concatenate([v["x_prompt"].reshape(TP, D), v["x_sample"].reshape(NS * TS, D)])
    c_rows = np.concatenate([v["c_prompt"], v["c_sample"]])
    par = np.concatenate(
        [_features(v[n]).reshape(P, -1) for n in ("g_pre_mix", "g_post_mix", "g_pre_ffn", "g_post_ffn", "b_a_dw",
                                                  "ln_a_g", "ln_a_b")]
        + [_features(v["g_kv"]).reshape(P, -1),
           _features(v["w_a_dw"][0]).transpose(0, 2, 1).reshape(P, -1),
           _features(v["b_ffn_dw"]).reshape(P, -1),
           _features(v["w_ffn_dw"]).transpose(0, 1, 3, 2).reshape(P, -1),
           _features(v["b_ada"]).reshape(P, -1)], axis=1)

    def alternate(a, b):
        return np.stack([_blocks(a, C, P), _blocks(b, C, P)], axis=1).reshape(-1, P, C * P)

    def up(layer, hf):
        w, n = v["w_ffn_up"][layer], FH * P
        return alternate(w[:, hf * n:(hf + 1) * n], w[:, FF + hf * n:FF + (hf + 1) * n])

    def wide_units(w):
        return w.reshape(4, 2, P, 2, 512).transpose(3, 0, 2, 1, 4).reshape(8, P, C * P)

    w_in, w_kv = v["w_a_in"][0], v["w_kv"]
    w_k8 = np.concatenate([alternate(w_in[:, D:], w_in[:, :D]), _blocks(v["w_a_out"][0], C, P), up(0, 0), up(0, 1),
                           _blocks(w_kv[:, :D], C, P), wide_units(w_kv[:, D:]), _blocks(v["w_q"][0], C, P),
                           _blocks(v["w_o"][0], C, P), up(1, 0), up(1, 1)])
    w_down = np.concatenate([_blocks(v["w_ffn_down"][layer][hf * FH * P:(hf + 1) * FH * P], FH, P)
                             for layer in range(DEPTH) for hf in range(2)])
    w_ada = np.concatenate([_blocks(v["w_ada"][layer], C, P) for layer in range(DEPTH)])
    arrays = {
        "x_in": _features(tokens).transpose(0, 2, 1),
        "c_in": _features(c_rows).transpose(0, 2, 1),
        "par_in": par,
        "b_sb_in": v["b_sb"].reshape(1, HEADS),
        "w_ada": w_ada,
        "w_k8": w_k8,
        "w_down": w_down,
        "state_a": _features(v["state_conv_a"][0]).transpose(0, 3, 1, 2).reshape(P, C * NS, WA - 1),
        "state_f": _features(v["state_ffn_conv"]).transpose(1, 0, 4, 2, 3).reshape(DEPTH, P, FC, NS * (WF - 1)),
        "cache_kt": v["cache_k"].reshape(N_PHYS, PAGE, PAIRS, P).transpose(0, 3, 2, 1),
        "cache_v": v["cache_v"].reshape(N_PHYS, PAGE, D),
        "page_table": v["page_table"].reshape(1, NS * PAGES).astype(np.int32),
    }
    arrays = {name: np.ascontiguousarray(a) for name, a in arrays.items()}
    nc = bacc.Bacc("TRN2", target_bir_lowering=False, num_devices=1)
    args = {name: nc.dram_tensor(f"{name}_dram", a.shape, mybir.dt.from_np(a.dtype), kind="ExternalInput").ap()
            for name, a in arrays.items()}
    outs = {name: nc.dram_tensor(f"{name}_dram", shape, F32, kind="ExternalOutput").ap() for name, shape in
            [(f"{n}_out", s) for n, s in _OUTS]}
    trunk_kernel(nc, *args.values(), *outs.values())
    r = run_bass_kernel_spmd(nc, [{f"{name}_dram": a for name, a in arrays.items()}], core_ids=[0])
    y, ca_p, ca_s, tails, k, val = (r.results[0][f"{n}_out_dram"] for n, _ in _OUTS)

    y = y.transpose(2, 1, 0).reshape(TT, D)
    k = k.transpose(2, 1, 0).reshape(TT, HEADS, HD)
    val = val.reshape(TT, HEADS, HD)
    ca_p = ca_p.transpose(2, 1, 0).reshape(1, 1, WA - 1, D)
    ca_s = ca_s.reshape(P, C, NS, WA - 1).transpose(2, 3, 1, 0).reshape(1, NS, WA - 1, D)
    tails = tails.reshape(DEPTH, P, FC, NB, 2).transpose(0, 3, 4, 2, 1).reshape(DEPTH, NB, 2, FF)
    return (y[:TP].reshape(1, TP, D), y[TP:].reshape(NS, TS, D), ca_p, ca_s, tails[:, :1], tails[:, 1:],
            k[:TP].reshape(1, TP, HEADS, HD), val[:TP].reshape(1, TP, HEADS, HD),
            k[TP:].reshape(NS, TS, HEADS, HD), val[TP:].reshape(NS, TS, HEADS, HD))
```

```python
from contextlib import ExitStack

import numpy as np

import concourse.bass as bass
from concourse import mybir

F32 = mybir.dt.float32
F32R = mybir.dt.float32r
BF16 = mybir.dt.bfloat16
I32 = mybir.dt.int32
ALU = mybir.AluOpType
ACT = mybir.ActivationFunctionType

P = 128
D = 1024
C = D // P
TP = 512
NS, TS = 8, 8
TT = TP + NS * TS
HALF = TT // 2
NB = 1 + NS
DEPTH = 2
FF = 2816
FC = FF // P
FH = FC // 2
HEADS, HD = 16, 64
PAIRS = HEADS // 2
WA = 31
WF = 3
PAGE = 128
PAGES = 4
N_PHYS = 40
MODS = 6 * C
EPS = 1e-6
KEY_COLS = TP + (TP - 128) + 128 + (TP - 256)
EXP_CAP = float(np.exp(40.0))

A_IN = (0, 8, C)
A_OUT = (16, 4, C)
UP = {(0, 0): (24, 11, C), (0, 1): (54, 11, C), (1, 0): (116, 11, C), (1, 1): (146, 11, C)}
DOWN = {(0, 0): (46, 4, FH), (0, 1): (76, 4, FH), (1, 0): (138, 4, FH), (1, 1): (168, 4, FH)}
KPROJ = (84, 4, C)
VPROJ = (92, 4, C)
QPROJ = (100, 4, C)
OPROJ = (108, 4, C)
UNITS = 176
PHASES = [A_IN, A_OUT, UP[0, 0], DOWN[0, 0], UP[0, 1], DOWN[0, 1], KPROJ, VPROJ, QPROJ, OPROJ,
          UP[1, 0], DOWN[1, 0], UP[1, 1], DOWN[1, 1]]

PAR = {}
_at = 0
for _name, _n in (("g_pre_mix", 2 * C), ("g_post_mix", 2 * C), ("g_pre_ffn", 2 * C), ("g_post_ffn", 2 * C),
                  ("b_a_dw", C), ("ln_a_g", C), ("ln_a_b", C), ("g_kv", C), ("w_a_dw", C * WA),
                  ("b_ffn_dw", 2 * FC), ("w_ffn_dw", 2 * FC * WF), ("b_ada", 2 * MODS)):
    PAR[_name] = _at
    _at += _n
N_PAR = _at

ADA_TILES = 4
GROUP = ADA_TILES * 4
GROUPS = DEPTH * MODS // GROUP
PIECES = 2 * C
ADA_RING = 4
DVE_CHUNKS = 6
LAG = 4
HN = 3
PE_TAPS = 6
CONSTS = 20
TAP_STEPS = WA - PE_TAPS + 1
SEQ_PART = 8
SEQ_STEPS = 14


H_FREE = ((0, 0), (2 * A_IN[1], 0), (A_OUT[0] + C, 0), (UP[0, 1][0] + FC, 0), (VPROJ[0] + 5, 1), (OPROJ[0] + C, 0))


def blocks(unit):
    for base, pairs, k in PHASES:
        if base <= unit < base + 2 * pairs:
            return k
    raise ValueError(unit)


def tiles_before(base):
    return base // 2 - (VPROJ[1] if base > VPROJ[0] else 0)


def trunk_kernel(nc, x_in, c_in, par_in, b_sb_in, w_ada, w_k8, w_down, state_a, state_f,
                 cache_kt, cache_v, page_table, y_out, conv_a_p, conv_a_s, ffn_tails, k_out, v_out):
    with ExitStack() as ctx:
        cursor = [16512]

        def place(name, shape, dtype=F32, at=None):
            size = int(np.prod(shape[1:])) * (2 if dtype == BF16 else 4)
            size = (size + 31) // 32 * 32
            here = cursor[0] if at is None else at[0]
            if at is None:
                cursor[0] += size
            else:
                at[0] += size
                assert at[0] <= at[1], (name, at)
            return nc.alloc_sbuf_tensor_at(name, shape, dtype, offset=here)

        def region(size):
            start = cursor[0]
            cursor[0] += size
            return lambda skip=0: [start + skip, start + size]

        def sem(name):
            return ctx.enter_context(nc.semaphore(name))

        x = place("x", [P, C, TT])
        raw = [place(f"raw{s}", [P, FH * P]) for s in range(2)]
        w_hi = [place(f"w_hi{s}", [P, FH * P], F32R) for s in range(2)]
        w_lo = [place(f"w_lo{s}", [P, FH * P], F32R) for s in range(2)]
        h_hi = place("h_hi", [P, C, TT], F32R)
        h_lo = place("h_lo", [P, C, TT], F32R)
        par = place("par", [P, N_PAR])
        bsb = place("bsb", [P, HEADS])
        bsb_sel = place("bsb_sel", [P, HEADS])
        bsb_row = place("bsb_row", [P, 1])
        one_row = place("one_row", [1, 64])
        mod = place("mod", [P, DEPTH, MODS, NB])
        a_mod = place("a_mod", [P, C, NB])
        g_mod = place("g_mod", [P, C, NB])
        no_shift = place("no_shift", [P, C, NB])
        mean_w = place("mean_w", [P, P])
        tri = place("tri", [P, P])
        neg_ones = place("neg_ones", [P, P])
        ident = place("ident", [P, P], BF16)
        mask = place("mask", [P, P], BF16)
        mask_new = place("mask_new", [P, NS * TS], BF16)
        ln_first = place("ln_first", [P, 1])
        eps_col = place("eps_col", [P, 1])
        rs_at = [cursor[0], cursor[0] + TT * 4]
        rs = place("rs", [P, TT])
        pages = place("pages", [1, NS * PAGES], I32)
        four_diag = place("four_diag", [P, ADA_TILES, NB])
        y = place("y", [P, C, TT])
        y_at = lambda: [y_off, y_off + C * TT * 4]
        y_off = cursor[0] - C * TT * 4

        wide = region(2 * FH * TT * 4)
        act_hi = place("act_hi", [P, FH, TT], F32R, at := wide())
        act_lo = place("act_lo", [P, FH, TT], F32R, at)
        u_p = place("u_p", [P, C, WA - 1 + TP], at=(at := wide()))
        u_s = place("u_s", [P, C, NS, WA - 1 + TS], at=at)
        c_raw = place("c_raw", [P, C, NB], at=at)
        ada_w = [place(f"ada_w{s}", [P, C * P], at=at) for s in range(ADA_RING)]
        diag = [place(f"diag{s}", [P, PE_TAPS, P], at=at) for s in range(2)]
        k_t = place("k_t", [P, PAIRS, TT], at=(at := wide()))
        v_n = place("v_n", [P, 5, D], at=at)
        k_st = place("k_st", [P, TP], at=at)
        v_st = place("v_st", [P, 4, P], at=at)
        q_st = place("q_st", [P, TP], at=rs_at)
        att_new = place("att_new", [64, 2, PAIRS, NS * TS], at=at)
        z_seq = place("z_seq", [P, TP], at=at)
        o_seq = place("o_seq", [P, 2 * P], at=at)
        ident_f = place("ident_f", [P, P], at=at)
        q_t = place("q_t", [P, PAIRS, TT], at=y_at())

        temp = region(229368 // 32 * 32 - cursor[0])
        at = temp()
        sq = place("sq", [P, 2, TT], at=at)
        hn = place("hn", [P, HN, TT], at=at)
        y_sum = place("y_sum", [P, TT], at=at)
        shared = at[0] - temp()[0]
        mu = place("mu", [P, TT], at=(at := temp(shared)))
        sig = place("sig", [P, TT], at=at)
        odd_taps = place("odd_taps", [P, TP], at=at)
        s_prod = place("s_prod", [P, SEQ_PART, NS, TS], at=at)
        s_sum = place("s_sum", [P, SEQ_PART, NS, TS], at=at)
        u_seq = place("u_seq", [P, NS, WA + TS], at=at)
        w_seq = place("w_seq", [P, WA + 2], at=at)
        mod_t = place("mod_t", [P, 4 * P], at=at)
        c_act = place("c_act", [P, C, 32], at=at)
        g_pad = place("g_pad", [P, WF - 1 + TP], at=(at := temp(shared)))
        g_seq = place("g_seq", [P, NS, WF - 1 + TS], at=at)
        cv = place("cv", [P, TT], at=at)
        val = place("val", [P, TT], at=at)
        ge = place("ge", [P, TT], at=at)
        prod = place("prod", [P, TT], at=at)
        tails = place("tails", [P, FC, (1 + NS) * 2], at=at)
        f_state = place("f_state", [P, FC, NS * 2], at=at)
        at = temp()
        att = [place(f"att{j}", [P, KEY_COLS], at=at) for j in range(2)]
        att_s = place("att_s", [P, PAGES * P], at=at)
        sp_new = place("sp_new", [64, 2, PAIRS, NS * TS], at=at)
        k_page = [place(f"k_page{t}", [P, PAIRS * PAGE], at=at) for t in range(PAGES)]
        v_page = [place(f"v_page{t}", [P, D], at=at) for t in range(2)]
        raw_at = [[16512 + C * TT * 4 + s * FH * P * 4, 16512 + C * TT * 4 + (s + 1) * FH * P * 4] for s in range(2)]
        v_page += [place(f"v_page{2 + s}", [P, D], at=raw_at[s]) for s in range(2)]
        q_seq = place("q_seq", [P, PAIRS, 4 * TS], at=raw_at[0])
        att_st = place("att_st", [64, P], at=raw_at[1])

        ps = ctx.enter_context(nc.psum_tensor("ps", [P, 8, 512], F32))

        def slot(s):
            return ps[:, 2 * s:2 * s + 2, 0:HALF]

        def two(ap):
            return ap.rearrange("p (b t) -> p b t", b=2)

        STAT = 2

        def prm(name, index, count=1):
            return par[:, bass.ds(PAR[name] + index, count)]

        def seq(ap):
            return ap.rearrange("p (s t) -> p s t", s=NS)

        def per_seq(tile, chunk):
            return tile[:, chunk, 1:NB].unsqueeze(2).to_broadcast([P, NS, TS])

        def chunk(tile, n, lo=0, hi=TT):
            return tile[:, bass.ds(n, 1), lo:hi].rearrange("p a t -> p (a t)")

        s_x, s_c, s_par, s_bsb, s_pages, s_state = (
            sem(n) for n in ("x_in", "c_in", "par_in", "bsb_in", "pages_in", "conv_state_in"))
        s_fstate = sem("ffn_state_in")
        s_const = sem("constants")
        w_in = [sem(f"w_in{s}") for s in range(2)]
        s_hi, s_lo, gemm_done = sem("w_hi_made"), sem("w_lo_made"), sem("unit_multiplied")
        slot_free = [sem(f"slot_free{s}") for s in range(2)]
        ada_in = [sem(f"ada_in{s}") for s in range(ADA_RING)]
        c_ready, ada_done, mod_ready, coef_ready = (
            sem(n) for n in ("c_silu", "ada_piece_done", "mod_ready", "coefficients"))
        mod_copied, mod_turned = sem("mod_rows_copied"), sem("mod_transposed")
        diag_made, taps_pe = sem("tap_diagonals_made"), sem("pe_taps_added")
        sq_ready, sq_used, stat_done, rs_ready, ln_step = (
            sem(n) for n in ("sq_ready", "sq_summed", "stat_done", "rs_ready", "rs_ln"))
        y_normed_p, x_ready_p = sem("y_normed_pool"), sem("x_ready_pool")
        y_sq, y_scaled, y_scaled_s, y_acc, y_normed, x_ready = (
            sem(n) for n in ("y_squared", "y_scaled", "y_scaled_seq", "y_sq_added", "y_normed", "x_ready"))
        hn_x, hn_p, hn_s, h_hi_ready, h_ready = (
            sem(n) for n in ("hn_x", "hn_prompt", "hn_seq", "h_hi_ready", "h_ready"))
        taps, conv_seq, conv_centred, pads_ready = (
            sem(n) for n in ("taps_added", "seq_taps_added", "conv_centred", "pads_zeroed"))
        gate_copied, cv_tap, conv_step, conv_done, gelu_done = (
            sem(n) for n in ("gate_copied", "cv_last_tap", "conv_step", "conv_done", "gelu_done"))
        state_put, tail_saved = sem("state_put"), sem("tail_saved")
        prod_done, act_hi_done, act_ready = sem("prod_done"), sem("act_hi_done"), sem("act_ready")
        v_act, v_dve = sem("v_read_act"), sem("v_read_dve")
        conv_stored, tails_stored, kv_stored, x_stored = (
            sem(n) for n in ("conv_stored", "tails_stored", "kv_stored", "x_stored"))
        bias_row = sem("bias_row_summed")
        buffers_free, new_step = sem("attention_buffers_free"), sem("new_step")
        k_in, v_in = ([sem(f"{n}_page_in{s}") for s in range(PAGES)] for n in "kv")
        k_used, k_staged, v_staged, q_staged, new_staged = (
            sem(n) for n in ("k_pages_used", "k_staged", "v_staged", "q_seq_staged", "att_new_staged"))
        z_done, exped, capped, lned, sp_done, suffixed, att_done, av_done = (
            sem(n) for n in ("z_done", "exp_done", "exp_capped", "ln_done", "softplus_done", "suffix_added",
                             "att_done", "av_done"))
        seq_z_copied, seq_turned, seq_exped, seq_capped, seq_lned, seq_sp = (
            sem(f"seq_{n}") for n in ("z_copied", "z_turned", "exp", "exp_capped", "ln", "softplus"))
        seq_suffixed, seq_att, seq_av, seq_o_copied, seq_o_turned = (
            sem(f"seq_{n}") for n in ("suffix_added", "att", "av", "o_copied", "o_turned"))
        seq_bank_free, pair_bank_free, seq_hi_done, pair_hi_done = (
            sem(n) for n in ("seq_bank_free", "pair_bank_free", "seq_o_hi", "pair_o_hi"))

        block = ctx.enter_context(nc.Block())

        def wait_stat(eng, index):
            if index % 2 == 0:
                eng.wait_ge(sq_used, C * (index // 2 + 1))
            else:
                eng.wait_ge(stat_done, (index + 1) // 2)

        def run_phase(eng, split, ph, even, odd, by=1):
            base, pairs, k = ph
            q0 = base // 2

            def call(handler, i, loop, n):
                if by == 1:
                    handler(i)
                else:
                    handler(i, n % 2, loop + (n + 1) // 2)

            split(q0 + 1, 0, k)
            call(even, 0, 0, 0)

            def body(loop):
                for n in range(by):
                    split(loop * by + (n + 1 + q0), 1, k)
                    call(odd, loop * by + n, loop, n)
                    split(loop * by + (n + 2 + q0), 0, k)
                    call(even, loop * by + (n + 1), loop, n + 1)

            if by > 1:
                body(0)
            with eng.Fori(by - 1, (pairs - 2) // by) as loop:
                body(loop)
            more = base + 2 * pairs < UNITS
            i = pairs - 1
            split(q0 + i, 1, k)
            call(odd, i - 1, (i - 1) // 2, (i - 1) % 2)
            if more:
                split(q0 + pairs, 0, blocks(base + 2 * pairs))
            call(even, i, i // 2, i % 2)
            call(odd, i, i // 2, i % 2)
            if more:
                split(q0 + pairs, 1, blocks(base + 2 * pairs))

        def fixed(i):
            return isinstance(i, int)

        def page_number(eng, i, t):
            index = PAGES * i + t
            return eng.value_load(pages[0:1, bass.ds(index, 1)], min_val=0, max_val=N_PHYS - 1)

        def page_load(eng, i, t, buffer, cache, arrived):
            page = page_number(eng, i, t)
            eng.dma_start(buffer[t][:], cache[bass.ds(page, 1)].rearrange("a p c -> (a p) c")).then_inc(arrived[t], 16)

        def z_cols(j):
            return ps[:].rearrange("p b c -> p (b c)")[:, 3 * j * 512:3 * j * 512 + KEY_COLS]

        def v_bank(half, t):
            return (5 * half + t) % 8

        def v_phase(split, v_half, step, steps):
            q0 = VPROJ[0] // 2
            split(q0 + 1, 0, C)
            split(q0 + 1, 1, C)
            split(q0 + 2, 0, C)
            split(q0 + 2, 1, C)
            v_half(0)
            for n, part in enumerate(steps):
                if n == 0:
                    split(q0 + 3, 0, C)
                elif n == 1:
                    split(q0 + 3, 1, C)
                elif n == 2:
                    split(QPROJ[0] // 2, 0, C)
                else:
                    v_half(1)
                    split(QPROJ[0] // 2, 1, C)
                for m in part:
                    step(m)

        @block.sync
        def _(sp):
            sp.dma_start(x[:], x_in).then_inc(s_x, 16)

            def ada_piece(n, s, first=False):
                if not first:
                    sp.wait_ge(ada_done, n - (ADA_RING - 1))
                sp.dma_start(ada_w[s][:], w_ada[bass.ds(n, 1)].rearrange("a p c -> (a p) c")).then_inc(ada_in[s], 16)

            def unit(q, s, src, row, n_cols):
                if not fixed(q) or q > 0:
                    sp.wait_ge(s_lo, 2 * q + (s - 1))
                sp.dma_start(raw[s][:, 0:n_cols], src[bass.ds(row, 1)].rearrange("a p c -> (a p) c"))\
                    .then_inc(w_in[s], 16)

            for n in range(PIECES):
                ada_piece(n, n % ADA_RING, n < ADA_RING)
            for s in range(2):
                unit(0, s, w_k8, s, C * P)
            with sp.Fori(0, A_IN[1]) as i:
                for s in range(2):
                    unit(i + 1, s, w_k8, 2 * i + (s + 2), C * P)
                    for j in range(PIECES // 4):
                        n = PIECES + PIECES // 4 * s + j
                        ada_piece(PIECES // 2 * i + n, n % ADA_RING)
            for n in range(PIECES * (GROUPS - 1), PIECES * GROUPS):
                ada_piece(n, n % ADA_RING)
            row = {C: 2 * A_IN[1], FH: 0}
            for ph in PHASES[1:]:
                base, pairs, k = ph
                skip = 1 if ph in (A_OUT, OPROJ) else 0
                src = w_k8 if k == C else w_down
                if ph == OPROJ:
                    for s in range(2):
                        unit(base // 2, s, src, row[k] + s, k * P)
                    sp.wait_ge(s_pages, 16)
                    sp.wait_ge(buffers_free, 1)
                    for t in range(PAGES):
                        page_load(sp, 0, t, k_page, cache_kt, k_in)
                    with sp.Fori(1, NS) as i:
                        sp.wait_ge(k_used, i)
                        for t in range(PAGES):
                            page_load(sp, i, t, k_page, cache_kt, k_in)
                    sp.wait_ge(seq_av, NS)
                with sp.Fori(skip, pairs) as i:
                    for s in range(2):
                        unit(i + base // 2, s, src, 2 * i + (row[k] + s), k * P)
                row[k] += 2 * pairs
            for n in sorted(range(C), key=lambda n: n % DVE_CHUNKS):
                if n < DVE_CHUNKS:
                    sp.wait_ge(x_ready, 3 * DVE_CHUNKS + n + 1)
                else:
                    sp.wait_ge(x_ready_p, 3 * (C - DVE_CHUNKS) + n - DVE_CHUNKS + 1)
                sp.dma_start(y_out[:, n, :], x[:, n, :]).then_inc(x_stored, 16)
            sp.wait_ge(x_stored, 16 * C)

        @block.tensor
        def _(pe):
            flat = ps[:].rearrange("p b c -> p (b c)")

            def block_passes(s, kb, k, hi, lo):
                for n, (w, v) in enumerate(((w_hi, hi), (w_hi, lo), (w_lo, hi))):
                    for b in range(2):
                        mm = pe.matmul(ps[:, 2 * s + b, 0:HALF], lhsT=w[s][:, kb * P:(kb + 1) * P],
                                       rhs=v[:, kb, b * HALF:(b + 1) * HALF],
                                       start=(kb == 0 and n == 0), stop=(kb == k - 1 and n == 2))
                return mm

            def gemm_unit(q, s, k, hi, lo, tiles, ready=None):
                pe.wait_ge(s_lo, 2 * q + (s + 1))
                pe.wait_ge(slot_free[s], tiles)
                for kb in range(k):
                    if ready is not None:
                        pe.wait_ge(ready[0], ready[1] + kb + 1)
                    mm = block_passes(s, kb, k, hi, lo)
                mm.then_inc(gemm_done, 1)

            def first_pair(q, k, tiles, ready):
                pe.wait_ge(s_lo, 2 * q + 2)
                if tiles > 0:
                    pe.wait_ge(slot_free[0], tiles)
                    pe.wait_ge(slot_free[1], tiles)
                for n in range(k + LAG):
                    if n < k:
                        pe.wait_ge(h_ready, ready + n + 1)
                    for s, kb in ((0, n), (1, n - LAG)):
                        if 0 <= kb < k:
                            mm = block_passes(s, kb, k, h_hi, h_lo)
                            if kb == k - 1:
                                mm.then_inc(gemm_done, 1)

            def phase(ph, hi, lo, ready=None, norm=None):
                base, pairs, k = ph
                q0, t0 = base // 2, tiles_before(base)
                if norm is not None:
                    first_pair(q0, k, t0, norm * C)
                else:
                    gemm_unit(q0, 0, k, hi, lo, t0, ready)
                    gemm_unit(q0, 1, k, hi, lo, t0)
                with pe.Fori(1, pairs) as i:
                    for s in range(2):
                        gemm_unit(i + q0, s, k, hi, lo, i + t0)

            def ada_piece(s, uses, kb, h):
                pe.wait_ge(ada_in[s], uses)
                for j in range(2):
                    t = 2 * h + j
                    mm = pe.matmul(ps[32 * t:32 * t + 32, 6, :], lhsT=c_act[:, kb, :], rhs=ada_w[s][:, j * 512:(j + 1) * 512],
                                   start=(kb == 0), stop=(kb == C - 1), skip_group_check=True)
                mm.then_inc(ada_done, 1)

            def turn_group(copied, read):
                pe.wait_ge(mod_copied, copied)
                if read is not None:
                    pe.wait_ge(mod_ready, read)
                for q in range(4):
                    mm = pe.matmul(ps[:, 7, q * ADA_TILES * NB:(q + 1) * ADA_TILES * NB], lhsT=mod_t[:, q * P:(q + 1) * P],
                                   rhs=four_diag[:].rearrange("p a b -> p (a b)"), start=(q == 0), stop=True,
                                   skip_group_check=True)
                mm.then_inc(mod_turned, 1)

            def stat_matmuls(src, start, stop):
                for b in range(2):
                    mm = pe.matmul(ps[:, 2 * STAT + b, 0:HALF], lhsT=mean_w[:], rhs=src[:, b * HALF:(b + 1) * HALF],
                                   start=start, stop=stop)
                return mm

            def squares_sum(index):
                if index:
                    pe.wait_ge(rs_ready, index)
                for n in range(C):
                    pe.wait_ge(sq_ready, C * (index // 2) + n + 1)
                    stat_matmuls(sq[:, n % 2, :], n == 0, n == C - 1).then_inc(sq_used, 1)

            def y_sum_stat(index, r):
                pe.wait_ge(rs_ready, index)
                pe.wait_ge(y_acc, (C + 1) * (r + 1))
                stat_matmuls(y_sum[:], True, True).then_inc(stat_done, 1)

            pe.wait_ge(s_const, CONSTS)
            squares_sum(0)
            pe.wait_ge(c_ready, 1)
            for n in range(PIECES):
                ada_piece(n % ADA_RING, 16 * (n // ADA_RING + 1), n // 2, n % 2)
            turn_group(1, None)

            def conv_taps(i, par):
                pe.wait_ge(slot_free[1], i + 1)
                pe.wait_ge(diag_made, PE_TAPS * (i + 1))
                if not fixed(i) or i >= 2:
                    pe.wait_ge(taps, TAP_STEPS * (i - 1))
                for k in range(PE_TAPS):
                    mm = pe.matmul(ps[:, 4 + par, :], lhsT=diag[par][:, k, :], rhs=chunk(u_p, i, k, k + TP),
                                   start=(k == 0), stop=(k == PE_TAPS - 1))
                mm.then_inc(taps_pe, 1)

            def half_group(g, par, s):
                for j in range(PIECES // 4):
                    n = PIECES // 2 * par + PIECES // 4 * s + j
                    ada_piece(n % ADA_RING, g * (16 * PIECES // ADA_RING) + 16 * (PIECES // ADA_RING + n // ADA_RING + 1),
                              n // 2, n % 2)

            def a_in_pair(i, par, g):
                gemm_unit(i, 0, C, h_hi, h_lo, i)
                if par == 0:
                    turn_group(g + 1, g)
                half_group(g, par, 0)
                conv_taps(i - 1, 1 - par)
                gemm_unit(i, 1, C, h_hi, h_lo, i)
                half_group(g, par, 1)

            first_pair(0, C, 0, 0)
            half_group(0, 0, 0)
            half_group(0, 0, 1)
            a_in_pair(1, 1, 0)
            a_in_pair(2, 0, 1)
            with pe.Fori(1, (A_IN[1] - 2) // 2) as j:
                a_in_pair(2 * j + 1, 1, j)
                a_in_pair(2 * j + 2, 0, j + 1)
            a_in_pair(A_IN[1] - 1, 1, A_IN[1] // 2 - 1)
            turn_group(GROUPS - 1, GROUPS - 2)
            def last_pieces(first, end):
                for n in range(first, end):
                    ada_piece(n % ADA_RING, 16 * (PIECES * (GROUPS - 1) // ADA_RING + n // ADA_RING + 1), n // 2, n % 2)

            last_pieces(0, 2)
            conv_taps(A_IN[1] - 1, 1)
            last_pieces(2, 7)
            pe.wait_ge(rs_ready, 1)
            pe.wait_ge(taps, TAP_STEPS * (C - 1) + 2)
            for n in range(C):
                pe.wait_ge(taps, TAP_STEPS * (n + 1))
                pe.wait_ge(conv_seq, SEQ_STEPS * (n + 1))
                mm = stat_matmuls(y[:, n, :], n == 0, n == C - 1)
            mm.then_inc(stat_done, 1)
            last_pieces(7, PIECES)
            squares_sum(2)
            phase(A_OUT, h_hi, h_lo, norm=1)
            y_sum_stat(3, 0)
            turn_group(GROUPS, GROUPS - 1)
            squares_sum(4)

            def ffn(layer, norm, r, index):
                phase(UP[layer, 0], h_hi, h_lo, norm=norm)
                phase(DOWN[layer, 0], act_hi, act_lo, (act_ready, 2 * layer * FH))
                phase(UP[layer, 1], h_hi, h_lo)
                phase(DOWN[layer, 1], act_hi, act_lo, (act_ready, (2 * layer + 1) * FH))
                y_sum_stat(index, r)

            ffn(0, 2, 1, 5)
            squares_sum(6)
            phase(KPROJ, h_hi, h_lo, norm=3)
            pe.wait_ge(rs_ready, 7)
            for s in range(2):
                pe.wait_ge(slot_free[s], VPROJ[0] // 2)
            for n in range(2 * VPROJ[1]):
                s = n % 2
                pe.wait_ge(s_lo, VPROJ[0] + n + 1)
                for j in range(2):
                    kb = 2 * (n % 4) + j
                    for t in range(5):
                        m = P if t < 4 else TT - 4 * P
                        if n == 4 and j == 0 and t == 3:
                            pe.wait_ge(v_act, 1)
                            pe.wait_ge(v_dve, 1)
                        for q, (a, w) in enumerate(((h_hi, w_hi), (h_lo, w_hi), (h_hi, w_lo))):
                            mm = pe.matmul(ps[0:m, v_bank(n // 4, t), :], lhsT=a[:, kb, t * P:t * P + m],
                                           rhs=w[s][:, j * 512:(j + 1) * 512],
                                           start=(kb == 0 and q == 0), stop=(kb == C - 1 and q == 2))
                mm.then_inc(gemm_done, 1)
            pe.wait_ge(v_act, 6)
            pe.wait_ge(v_dve, 4)
            phase(QPROJ, h_hi, h_lo, norm=4)

            for s in range(2):
                pe.wait_ge(slot_free[s], tiles_before(OPROJ[0]))
            for j in range(2):
                r = slice(HD * j, HD * j + HD)
                for p in range(PAIRS):
                    mm = pe.matmul(ps[0:64, j, p * 64:(p + 1) * 64], lhsT=k_t[r, p, TP:TT], rhs=q_t[r, p, TP:TT],
                                   start=(p == 0), stop=True, skip_group_check=True)
            mm.then_inc(new_step, 1)
            pe.wait_ge(new_step, 1)
            for j in range(2):
                pe.matmul(ps[0:64, j, :], lhsT=one_row[0:1, 0:64],
                          rhs=bsb[0:1, j:HEADS:2].unsqueeze(2).to_broadcast([1, PAIRS, 64]),
                          start=False, stop=True, skip_group_check=True)
                mm = pe.matmul(ps[0:64, j, :], lhsT=ident[0:64, 0:64],
                               rhs=mask_new[0:64, :].unsqueeze(1).to_broadcast([64, PAIRS, 64]),
                               start=False, stop=True, skip_group_check=True)
            mm.then_inc(new_step, 1)
            pe.wait_ge(new_step, 6)
            for j in range(2):
                mm = pe.matmul(ps[0:64, j, :], lhsT=tri[0:64, 0:64], rhs=sp_new[:, j].rearrange("p a q -> p (a q)"),
                               start=False, stop=True, skip_group_check=True)
            mm.then_inc(new_step, 1)
            pe.wait_ge(new_step, 8)
            pe.wait_ge(mod_ready, GROUPS)

            def chunk_cols(c):
                return ((0, 512), (512, 384), (1024, 256), (896, 128))[c]

            def z_head(j, i):
                r, b0 = slice(HD * j, HD * j + HD), 3 * j * 512
                pe.wait_ge(k_staged, 4 * i + (2 * j + 2))
                if not fixed(i) or i > 0:
                    pe.wait_ge(att_done, 2 * i + (j - 1))
                for c in range(4):
                    at, n = chunk_cols(c)
                    pe.matmul(flat[:, b0 + at:b0 + at + n], lhsT=k_st[r, c * P:(c + 1) * P],
                              rhs=q_st[r, c * P:TP],
                              start=(c != 3), stop=True, skip_group_check=True)
                for c in range(4):
                    at, n = chunk_cols(c)
                    mm = pe.matmul(flat[:, b0 + at:b0 + at + P], lhsT=ident[:], rhs=mask[:],
                                   start=False, stop=True, skip_group_check=True)
                mm.then_inc(z_done, 1)

            def suffix_head(j, i):
                pe.wait_ge(sp_done, 2 * i + (j + 1))
                b0 = 3 * j * 512
                for c in range(4):
                    at, n = chunk_cols(c)
                    for c2 in range(c, 4):
                        at2, n2 = chunk_cols(c2)
                        mm = pe.matmul(flat[:, b0 + at + (c2 - c) * P:b0 + at + n],
                                       lhsT=(tri if c2 == c else neg_ones)[:], rhs=att[j][:, at2:at2 + n2],
                                       start=False, stop=True, skip_group_check=True)
                mm.then_inc(suffixed, 1)

            def av_head(j, i):
                pe.wait_ge(att_done, 2 * i + (j + 1))
                pe.wait_ge(v_staged, 2 * i + (j + 1))
                for c in range(4):
                    at, n = chunk_cols(c)
                    mm = pe.matmul(ps[HD * j:HD * j + HD, 6, c * P:TP], lhsT=v_st[:, c, HD * j:HD * j + HD],
                                   rhs=att[j][:, at:at + n], start=(c == 0), stop=(c == 3), skip_group_check=True)
                mm.then_inc(av_done, 1)

            def seq_scores(i):
                pe.wait_ge(q_staged, 4 * i + 4)
                if not fixed(i) or i > 0:
                    pe.wait_ge(seq_bank_free, i)
                for t in range(PAGES):
                    pe.wait_ge(k_in[t], 16 * i + 16)
                    for a in range(2):
                        for j in range(4):
                            p = 2 * j + a
                            mm = pe.matmul(ps[32 * j:32 * j + 32, 7, t * PAGE:(t + 1) * PAGE], lhsT=q_seq[:, p, :],
                                           rhs=k_page[t][:, p * PAGE:(p + 1) * PAGE], start=(t == 0 and a == 0),
                                           stop=(a == 1), skip_group_check=True)
                mm.then_inc(k_used, 1)

            def turn_scores(i):
                pe.wait_ge(seq_z_copied, i + 1)
                for c in range(4):
                    mm = pe.matmul(ps[:, 7, c * P:(c + 1) * P], lhsT=z_seq[:, c * P:(c + 1) * P], rhs=ident_f[:],
                                   start=(c == 0), stop=True, skip_group_check=True)
                mm.then_inc(seq_turned, 1)

            def seq_suffix(i):
                pe.wait_ge(seq_sp, i + 1)
                for c in range(4):
                    for c2 in range(c, 4):
                        pe.matmul(ps[:, 7, c * P:(c + 1) * P], lhsT=(tri if c2 == c else neg_ones)[:],
                                  rhs=att_s[:, c2 * P:(c2 + 1) * P], start=False, stop=True, skip_group_check=True)
                    for j in range(2):
                        out = ps[:, 7, c * P:(c + 1) * P].rearrange("p (a j q) -> p a j q", j=2, q=TS)[:, :, j]
                        mm = pe.matmul(out, lhsT=neg_ones[0:64, :], rhs=sp_new[:, j, :, bass.ds(i * TS, TS)],
                                       start=False, stop=True, skip_group_check=True)
                mm.then_inc(seq_suffixed, 1)

            def seq_output(i):
                pe.wait_ge(seq_att, i + 1)
                pe.wait_ge(new_staged, i + 1)
                for c in range(PAGES + 1):
                    if c < PAGES:
                        pe.wait_ge(v_in[c], 16 * i + 16)
                    for j in range(4):
                        w = att_s[:, c * P + 32 * j:c * P + 32 * j + 32] if c < PAGES else att_st[:, 32 * j:32 * j + 32]
                        v = v_page[c][:, 256 * j:256 * j + 256] if c < PAGES else v_n[0:64, 4, 256 * j:256 * j + 256]
                        mm = pe.matmul(ps[32 * j:32 * j + 32, 7, 0:256], lhsT=w, rhs=v, start=(c == 0),
                                       stop=(c == PAGES), skip_group_check=True)
                mm.then_inc(seq_av, 1)

            def turn_output(i):
                pe.wait_ge(seq_o_copied, i + 1)
                columns = ident_f[:].rearrange("p (j a b) -> p j a b", a=2, b=2 * TS)
                for a in range(2):
                    mm = pe.matmul(ps[:, 7, 256 + 64 * a:320 + 64 * a], lhsT=o_seq[:, a * P:(a + 1) * P],
                                   rhs=columns[:, :, a], start=(a == 0), stop=True, skip_group_check=True)
                mm.then_inc(seq_o_turned, 1)

            def finish_pair(i):
                suffix_head(1, i)
                seq_output(i)
                av_head(1, i)
                turn_output(i)

            def rest_of_pair(i):
                suffix_head(0, i)
                seq_scores(i)
                z_head(1, i)
                turn_scores(i)
                if not fixed(i) or i > 0:
                    pe.wait_ge(pair_bank_free, i)
                av_head(0, i)

            z_head(0, 0)
            rest_of_pair(0)
            with pe.Fori(1, PAIRS) as i:
                z_head(0, i)
                seq_suffix(i - 1)
                finish_pair(i - 1)
                rest_of_pair(i)
            seq_suffix(PAIRS - 1)
            finish_pair(PAIRS - 1)
            pe.wait_ge(seq_bank_free, NS)
            pe.wait_ge(pair_bank_free, PAIRS)
            phase(OPROJ, h_hi, h_lo)
            y_sum_stat(7, 2)
            squares_sum(8)
            ffn(1, 5, 3, 9)

        @block.scalar
        def _(act):
            act.dma_start(c_raw[:], c_in).then_inc(s_c, 16)
            act.dma_start(par[:], par_in).then_inc(s_par, 16)
            act.wait_ge(s_c, 16)
            act.wait_ge(pads_ready, 1)
            act.activation(c_act[:, :, 0:NB], c_raw[:], ACT.Silu).then_inc(c_ready, 1)

            def split(q, s, k):
                act.wait_ge(w_in[s], 16 * q + 16)
                if not fixed(q) or q > 0:
                    act.wait_ge(gemm_done, 2 * q + (s - 1))
                act.activation(w_hi[s][:, 0:k * P], raw[s][:, 0:k * P], ACT.Copy).then_inc(s_hi, 1)

            def rms(index):
                act.activation(ln_first[:], eps_col[:], ACT.Ln)
                wait_stat(act, index)
                act.activation(two(rs[:]), slot(STAT), ACT.Ln, bias=eps_col[:, 0:1]).then_inc(ln_step, 1)
                act.wait_ge(ln_step, max(index, 1))
                act.activation(rs[:], rs[:], ACT.Exp, scale=-0.5).then_inc(rs_ready, 1)

            def squares(norm, src, ready=None, r=None):
                for n in range(C):
                    if ready is not None:
                        act.wait_ge(ready, n + 1)
                    if r is not None and n < DVE_CHUNKS:
                        act.wait_ge(x_ready, r * DVE_CHUNKS + n + 1)
                    elif r is not None:
                        act.wait_ge(x_ready_p, r * (C - DVE_CHUNKS) + n - DVE_CHUNKS + 1)
                    if n >= 2:
                        act.wait_ge(sq_used, norm * C + n - 1)
                    act.activation(sq[:, n % 2, :], src[:, n, :], ACT.Square).then_inc(sq_ready, 1)

            def modulate_step(norm, shift=None, at=0):
                def hi(n):
                    act.wait_ge(hn_p, norm * C + n + 1)
                    if shift is not None:
                        act.wait_ge(hn_s, 2 * ((norm if norm == 0 else norm - 1) * C + n + 1))
                    if H_FREE[norm][0]:
                        act.wait_ge(gemm_done, H_FREE[norm][0] + n // 2 * H_FREE[norm][1])
                    act.activation(h_hi[:, n, :], hn[:, n % HN, :], ACT.Copy).then_inc(h_hi_ready, 1)

                def step(n):
                    if n < C:
                        act.wait_ge(hn_x, norm * C + n + 1)
                        if shift is None:
                            act.activation(hn[:, n % HN, :], hn[:, n % HN, :], ACT.Silu, bias=prm("ln_a_b", n),
                                           scale=prm("ln_a_g", n)).then_inc(hn_p, 1)
                        else:
                            act.activation(hn[:, n % HN, 0:TP], hn[:, n % HN, 0:TP], ACT.Identity,
                                           bias=shift[:, at + n, 0:1], scale=a_mod[:, n, 0:1]).then_inc(hn_p, 1)
                    if n:
                        hi(n - 1)

                return step

            def modulate(norm, shift=None, at=0):
                step = modulate_step(norm, shift, at)
                for n in range(C + 1):
                    step(n)

            act.wait_ge(s_const, CONSTS)
            act.wait_ge(s_par, 16)
            act.wait_ge(s_x, 16)
            squares(0, x)
            rms(0)
            split(0, 0, C)
            split(0, 1, C)

            def copy_group(g):
                act.wait_ge(ada_done, PIECES * (g + 1))
                if not fixed(g) or g > 0:
                    act.wait_ge(mod_turned, g)
                act.activation(mod_t[:], ps[:, 6, :], ACT.Copy).then_inc(mod_copied, 1)

            copy_group(0)
            modulate(0, mod[:, 0], 0)

            def gate_a(i, par, _):
                act.wait_ge(gemm_done, 2 * i + 1)
                if not fixed(i) or i > 0:
                    act.wait_ge(slot_free[1], i)
                act.activation(two(sig[:]), slot(0), ACT.Sigmoid).then_inc(slot_free[0], 1)
                if not fixed(i) or i >= 2:
                    act.wait_ge(taps_pe, i - 1)
                for k in range(PE_TAPS):
                    act.activation(diag[par][:, k, :], ident[:], ACT.Copy, scale=prm("w_a_dw", i * WA + k))\
                        .then_inc(diag_made, 1)

            def after_a(i, par, g):
                if par == 1:
                    copy_group(g)

            run_phase(act, split, A_IN, gate_a, after_a, by=2)

            wait_stat(act, 1)
            act.activation(two(mu[:]), slot(STAT), ACT.Copy).then_inc(rs_ready, 1)
            squares(1, y, ready=conv_centred)
            rms(2)
            modulate(1)
            copy_group(GROUPS - 1)

            def finish(r, ph, copy):
                def handler(i, s):
                    m = 2 * i + s
                    if copy:
                        act.wait_ge(gemm_done, m + (ph[0] + 1))
                    else:
                        act.wait_ge(slot_free[s], i + (tiles_before(ph[0]) + 1))
                    if not fixed(m) or m >= 2:
                        act.wait_ge(y_acc, 2 * i + (s + r * (C + 1)))
                    if copy:
                        act.activation(two(sq[:, s, :]), slot(s), ACT.Square).then_inc(y_sq, 1)
                        act.activation(two(chunk(y, 2 * i + s)), slot(s), ACT.Copy).then_inc(slot_free[s], 1)
                        act.wait_ge(slot_free[s], i + (tiles_before(ph[0]) + 1))
                    else:
                        act.activation(sq[:, s, :], chunk(y, 2 * i + s), ACT.Square).then_inc(y_sq, 1)
                        act.wait_ge(y_sq, m + (r * C + 1))
                    act.activation(chunk(y, m, 0, TP), chunk(y, m, 0, TP), ACT.Copy, scale=chunk(g_mod, m, 0, 1))\
                        .then_inc(y_scaled, 1)
                return (lambda i: handler(i, 0)), (lambda i: handler(i, 1))

            act.wait_ge(coef_ready, 2)
            run_phase(act, split, A_OUT, *finish(0, A_OUT, True))
            rms(3)
            squares(2, x, r=0)
            rms(4)
            modulate(2, mod[:, 0], 3 * C)

            def ffn(layer, r):
                for hf in range(2):
                    ph = UP[layer, hf]
                    g0 = (2 * layer + hf) * FH
                    f0 = layer * FC + hf * FH

                    def gate_f(i):
                        g = i + g0
                        act.wait_ge(gemm_done, 2 * i + (ph[0] + 1))
                        if not fixed(g) or g > 0:
                            act.wait_ge(conv_done, g)
                            act.wait_ge(tail_saved, 2 * g)
                        act.activation(g_pad[:, 2:2 + HALF], ps[:, 0, 0:HALF], ACT.Copy)
                        act.activation(g_pad[:, 2 + HALF:2 + TP], ps[:, 1, 0:TP - HALF], ACT.Copy)
                        act.activation(g_seq[:, :, 2:2 + TS], seq(ps[:, 1, TP - HALF:HALF]), ACT.Copy)\
                            .then_inc(gate_copied, 1)

                    def value_f(i):
                        g = i + g0
                        act.wait_ge(gemm_done, 2 * i + (ph[0] + 2))
                        if not fixed(g) or g > 0:
                            act.wait_ge(prod_done, g)
                        act.activation(two(val[:]), slot(1), ACT.Copy).then_inc(slot_free[1], 1)
                        act.wait_ge(conv_done, g + 1)
                        act.activation(ge[:], cv[:], ACT.Gelu_apprx_tanh).then_inc(gelu_done, 1)

                    run_phase(act, split, ph, gate_f, value_f)
                    down = DOWN[layer, hf]
                    if hf == 0:
                        def part(i, s):
                            act.wait_ge(gemm_done, 2 * i + (down[0] + s + 1))
                            act.activation(two(chunk(y, 2 * i + s)), slot(s), ACT.Copy).then_inc(slot_free[s], 1)
                        run_phase(act, split, down, lambda i: part(i, 0), lambda i: part(i, 1))
                    else:
                        run_phase(act, split, down, *finish(r, down, False))

            ffn(0, 1)
            rms(5)
            squares(3, x, r=1)
            rms(6)
            modulate(3, no_shift, 0)

            def projected(ph, dst, scale):
                def handler(i, s):
                    act.wait_ge(gemm_done, 2 * i + (ph[0] + s + 1))
                    act.activation(two(chunk(dst, 2 * i + s)), slot(s), ACT.Copy, scale=scale)\
                        .then_inc(slot_free[s], 1)
                return (lambda i: handler(i, 0)), (lambda i: handler(i, 1))

            run_phase(act, split, KPROJ, *projected(KPROJ, k_t, 1.0))

            def v_half(hf):
                act.wait_ge(gemm_done, VPROJ[0] + 4 * hf + 4)
                for t in (0, 2, 4):
                    m = P if t < 4 else TT - 4 * P
                    act.activation(v_n[0:m, t, hf * 512:(hf + 1) * 512], ps[0:m, v_bank(hf, t), :], ACT.Copy)\
                        .then_inc(v_act, 1)

            v_phase(split, v_half, modulate_step(4, mod[:, 1], 0), ((0, 1, 2), (3, 4), (5, 6), (7, 8)))
            run_phase(act, split, QPROJ, *projected(QPROJ, q_t, HD ** -0.5))

            act.wait_ge(buffers_free, 1)
            act.wait_ge(new_step, 2)
            act.activation(sp_new[:].rearrange("p j a q -> p j (a q)"), ps[0:64, 0:2, :], ACT.Exp).then_inc(new_step, 1)
            act.wait_ge(new_step, 4)
            act.activation(sp_new[:], sp_new[:], ACT.Ln, bias=1.0).then_inc(new_step, 1)
            act.wait_ge(new_step, 7)
            act.activation(att_new[:].rearrange("p j a q -> p j (a q)"), ps[0:64, 0:2, :], ACT.Exp)\
                .then_inc(new_step, 1)

            def first_exp(j, i):
                act.wait_ge(z_done, 2 * i + (j + 1))
                act.activation(att[j][:], z_cols(j), ACT.Exp, bias=bsb[:, bass.ds(2 * i + j, 1)]).then_inc(exped, 1)

            def ln(j, i):
                act.wait_ge(capped, 2 * i + (j + 1))
                act.activation(att[j][:], att[j][:], ACT.Ln, bias=1.0).then_inc(lned, 1)

            def weights(j, i):
                act.wait_ge(suffixed, 2 * i + (j + 1))
                act.activation(att[j][:], z_cols(j), ACT.Exp, bias=bsb[:, bass.ds(i + i + j, 1)]).then_inc(att_done, 1)

            def finish_pair(i):
                act.wait_ge(seq_suffixed, i + 1)
                act.activation(att_s[:], ps[:, 7, :], ACT.Exp).then_inc(seq_att, 1)
                weights(1, i)

            def rest_of_pair(i):
                ln(0, i)
                weights(0, i)
                act.wait_ge(k_used, i + 1)
                act.activation(z_seq[:], ps[:, 7, :], ACT.Identity, bias=bsb_row[:]).then_inc(seq_z_copied, 1)
                first_exp(1, i)
                act.wait_ge(seq_turned, i + 1)
                act.activation(att_s[:], ps[:, 7, :], ACT.Exp).then_inc(seq_exped, 1)
                ln(1, i)
                act.wait_ge(seq_capped, i + 1)
                act.activation(att_s[:], att_s[:], ACT.Ln, bias=1.0).then_inc(seq_lned, 1)

            act.wait_ge(bias_row, 1)
            first_exp(0, 0)
            rest_of_pair(0)
            with act.Fori(1, PAIRS) as i:
                first_exp(0, i)
                finish_pair(i - 1)
                rest_of_pair(i)
            finish_pair(PAIRS - 1)

            act.wait_ge(coef_ready, 7)
            run_phase(act, split, OPROJ, *finish(2, OPROJ, True))
            rms(7)
            squares(4, x, r=2)
            rms(8)
            modulate(5, mod[:, 1], 3 * C)
            ffn(1, 3)
            rms(9)

        @block.vector
        def _(dve):
            def split(q, s, k):
                dve.wait_ge(s_hi, 2 * q + (s + 1))
                dve.tensor_tensor(w_lo[s][:, 0:k * P], raw[s][:, 0:k * P], w_hi[s][:, 0:k * P].bitcast(F32),
                                  ALU.subtract).then_inc(s_lo, 1)

            def scale_coef(l, at, gain):
                dve.scalar_tensor_tensor(out=a_mod[:], in0=mod[:, l, at:at + C, :], scalar=1.0, in1=gain_of(gain, l),
                                         op0=ALU.add, op1=ALU.mult).then_inc(coef_ready, 1)

            def gate_coef(l, at, gain):
                dve.tensor_tensor(g_mod[:], mod[:, l, at:at + C, :], gain_of(gain, l), ALU.mult)\
                    .then_inc(coef_ready, 1)

            def gain_of(name, l):
                return par[:, PAR[name] + l * C:PAR[name] + (l + 1) * C].unsqueeze(2).to_broadcast([P, C, NB])

            def bias_mod(g):
                def of_group(tile, first, width):
                    return tile[:, bass.ds(g * (GROUP * width) + first, GROUP * width)]

                b = of_group(par, PAR["b_ada"], 1).rearrange("p (t q) -> p t q", q=4)\
                    .unsqueeze(3).to_broadcast([P, ADA_TILES, 4, NB])
                out = of_group(mod[:].rearrange("p l c b -> p (l c b)"), 0, NB)\
                    .rearrange("p (t q b) -> p t q b", q=4, b=NB)
                src = ps[:, 7, 0:GROUP * NB].rearrange("p (q t b) -> p t q b", q=4, b=NB)
                dve.wait_ge(mod_turned, g + 1)
                dve.tensor_tensor(out, src, b, ALU.add).then_inc(mod_ready, 1)

            def norm_step(norm, src, index):
                def step(n):
                    if n == 0:
                        dve.wait_ge(rs_ready, index + 1)
                    if n < C:
                        if n >= HN:
                            dve.wait_ge(h_ready, norm * C + n - HN + 1)
                        dve.tensor_tensor(hn[:, n % HN, :], src[:, n, :], rs[:], ALU.mult).then_inc(hn_x, 1)
                    if n >= 2:
                        m = n - 2
                        dve.wait_ge(h_hi_ready, norm * C + m + 1)
                        dve.tensor_tensor(h_lo[:, m, :], hn[:, m % HN, :], h_hi[:, m, :].bitcast(F32), ALU.subtract)\
                            .then_inc(h_ready, 1)

                return step

            def apply_norm(norm, src, index):
                step = norm_step(norm, src, index)
                for n in range(C + 2):
                    step(n)

            def residual(r, index):
                dve.wait_ge(rs_ready, index + 1)

                def add(n):
                    dve.wait_ge(y_normed, r * DVE_CHUNKS + n + 1)
                    dve.tensor_tensor(x[:, n, :], x[:, n, :], y[:, n, :], ALU.add).then_inc(x_ready, 1)

                for n in range(DVE_CHUNKS):
                    dve.wait_ge(y_scaled, r * C + n + 1)
                    dve.wait_ge(y_scaled_s, r * C + n + 1)
                    dve.tensor_tensor(y[:, n, :], y[:, n, :], rs[:], ALU.mult).then_inc(y_normed, 1)
                    if n:
                        add(n - 1)
                add(DVE_CHUNKS - 1)

            dve.wait_ge(s_par, 16)
            split(0, 0, C)
            split(0, 1, C)
            bias_mod(0)
            dve.wait_ge(mod_ready, 1)
            scale_coef(0, C, "g_pre_mix")
            apply_norm(0, x, 0)

            def tap(i, n, bank=None):
                g = TAP_STEPS * i
                if n:
                    dve.wait_ge(taps, g + (n - 1))
                elif not fixed(i) or i > 0:
                    dve.wait_ge(taps, g)
                k = PE_TAPS + n
                out = odd_taps[:] if n % 2 else chunk(y, i, 0, TP)
                src = chunk(u_p, i, k, k + TP) if k < WA else None
                if k == WA:
                    out = chunk(y, i, 0, TP)
                    dve.wait_ge(taps, g + n)
                    ins = dve.tensor_tensor(out, out, odd_taps[:], ALU.add)
                elif n == 0:
                    ins = dve.tensor_scalar(out, src, prm("w_a_dw", i * WA + k), prm("b_a_dw", i), ALU.mult, ALU.add)
                else:
                    if n == 1:
                        dve.wait_ge(taps_pe, i + 1)
                    ins = dve.scalar_tensor_tensor(out=out, in0=src, scalar=prm("w_a_dw", i * WA + k),
                                                   in1=ps[:, bank, :] if n == 1 else out,
                                                   op0=ALU.mult, op1=ALU.add)
                ins.then_inc(taps, 1)

            early = (WA - PE_TAPS) // 2

            def glu(i, par, _):
                dve.wait_ge(slot_free[0], i + 1)
                dve.wait_ge(gemm_done, 2 * i + 2)
                parts = ((chunk(u_p, i, WA - 1, WA - 1 + HALF), ps[:, 2, 0:HALF], sig[:, 0:HALF]),
                         (chunk(u_p, i, WA - 1 + HALF, WA - 1 + TP), ps[:, 3, 0:TP - HALF], sig[:, HALF:TP]),
                         (u_s[:, bass.ds(i, 1), :, WA - 1:WA - 1 + TS].rearrange("p a s t -> p (a s) t"),
                          seq(ps[:, 3, TP - HALF:HALF]), seq(sig[:, TP:TT])))
                for out, a, b in parts:
                    ins = dve.tensor_tensor(out, a, b, ALU.mult)
                ins.then_inc(slot_free[1], 1)
                if fixed(i) and i == 0:
                    return
                for n in range(early, TAP_STEPS):
                    tap(i - 1, n)

            def early_taps(i, par):
                if fixed(i) and i == 0:
                    return
                dve.wait_ge(slot_free[1], i)
                for n in range(early):
                    tap(i - 1, n, 5 - par)

            def taps_and_mod(i, par, g):
                early_taps(i, par)
                if par == 0 and not (fixed(i) and i == 0):
                    bias_mod(g)

            dve.wait_ge(pads_ready, 2)
            run_phase(dve, split, A_IN, taps_and_mod, glu, by=2)
            early_taps(A_IN[1], 0)
            for n in range(early, TAP_STEPS):
                tap(A_IN[1] - 1, n)
            bias_mod(GROUPS - 2)
            dve.wait_ge(mod_ready, GROUPS - 1)
            gate_coef(0, 2 * C, "g_post_mix")
            dve.wait_ge(rs_ready, 2)
            for n in range(C):
                dve.tensor_tensor(y[:, n, :], y[:, n, :], mu[:], ALU.subtract).then_inc(conv_centred, 1)
            apply_norm(1, y, 2)
            dve.wait_ge(conv_stored, 32)

            def y_squares(r, ph, add):
                def handler(i, s):
                    if add:
                        dve.wait_ge(gemm_done, 2 * i + (ph[0] + s + 1))
                        yc = two(chunk(y, 2 * i + s))
                        dve.tensor_tensor(yc, slot(s), yc, ALU.add).then_inc(slot_free[s], 1)
                    if s == 1:
                        acc(2 * i, 0)
                    elif not fixed(i) or i > 0:
                        acc(2 * i - 1, 1)

                def acc(m, s):
                    dve.wait_ge(y_sq, m + (r * C + 1))
                    dve.wait_ge(y_acc, m + (r * (C + 1) + 1))
                    dve.tensor_tensor(y_sum[:], y_sum[:], sq[:, s, :], ALU.add).then_inc(y_acc, 1)

                dve.memset(y_sum[:], 0.0).then_inc(y_acc, 1)
                run_phase(dve, split, ph, lambda i: handler(i, 0), lambda i: handler(i, 1))
                acc(C - 1, 1)

            y_squares(0, A_OUT, False)
            scale_coef(0, 4 * C, "g_pre_ffn")
            residual(0, 3)
            apply_norm(2, x, 4)
            bias_mod(GROUPS - 1)

            def ffn(layer, r):
                gate_coef(layer, 5 * C, "g_post_ffn")
                for hf in range(2):
                    ph = UP[layer, hf]
                    g0 = (2 * layer + hf) * FH
                    f0 = layer * FC + hf * FH

                    def conv(i):
                        g = i + g0
                        dve.wait_ge(gate_copied, g + 1)
                        if not fixed(g) or g > 0:
                            dve.wait_ge(gelu_done, g)
                        dve.wait_ge(state_put, g + 1)
                        w, b = prm("w_ffn_dw", (i + f0) * WF + 2), prm("b_ffn_dw", i + f0)
                        dve.tensor_scalar(cv[:, 0:TP], g_pad[:, 2:2 + TP], w, b, ALU.mult, ALU.add)\
                            .then_inc(slot_free[0], 1)
                        dve.tensor_scalar(seq(cv[:, TP:TT]), g_seq[:, :, 2:2 + TS], w, b, ALU.mult, ALU.add)\
                            .then_inc(cv_tap, 1)
                        dve.wait_ge(cv_tap, g + 1)
                        for j in (1, 0):
                            w = prm("w_ffn_dw", (i + f0) * WF + j)
                            if j == 0:
                                dve.wait_ge(conv_step, 3 * g + 2)
                            dve.scalar_tensor_tensor(out=cv[:, 0:TP], in0=g_pad[:, j:j + TP], scalar=w,
                                                     in1=cv[:, 0:TP], op0=ALU.mult, op1=ALU.add).then_inc(conv_step, 1)
                            last = dve.scalar_tensor_tensor(out=seq(cv[:, TP:TT]), in0=g_seq[:, :, j:j + TS],
                                                            scalar=w, in1=seq(cv[:, TP:TT]), op0=ALU.mult,
                                                            op1=ALU.add)
                            last.then_inc(conv_step if j else conv_done, 1)

                    def gated(i):
                        g = i + g0
                        dve.wait_ge(gelu_done, g + 1)
                        if not fixed(g) or g > 0:
                            dve.wait_ge(act_ready, g)
                        dve.tensor_tensor(prod[:], ge[:], val[:], ALU.mult).then_inc(prod_done, 1)
                        dve.wait_ge(prod_done, g + 1)
                        dve.tensor_copy(chunk(act_hi, i), prod[:]).then_inc(act_hi_done, 1)
                        dve.wait_ge(act_hi_done, g + 1)
                        dve.tensor_tensor(chunk(act_lo, i), prod[:], chunk(act_hi, i).bitcast(F32), ALU.subtract)\
                            .then_inc(act_ready, 1)

                    run_phase(dve, split, ph, conv, gated)
                    if hf == 0:
                        run_phase(dve, split, DOWN[layer, 0], lambda i: None, lambda i: None)
                    else:
                        y_squares(r, DOWN[layer, 1], True)

            ffn(0, 1)
            dve.tensor_copy(a_mod[:], par[:, PAR["g_kv"]:PAR["g_kv"] + C].unsqueeze(2).to_broadcast([P, C, NB]))\
                .then_inc(coef_ready, 1)
            residual(1, 5)
            apply_norm(3, x, 6)
            run_phase(dve, split, KPROJ, lambda i: None, lambda i: None)

            def v_half(hf):
                dve.wait_ge(gemm_done, VPROJ[0] + 4 * hf + 4)
                for t in (1, 3):
                    dve.tensor_copy(v_n[:, t, hf * 512:(hf + 1) * 512], ps[:, v_bank(hf, t), :]).then_inc(v_dve, 1)

            scale_coef(1, C, "g_pre_mix")
            v_phase(split, v_half, norm_step(4, x, 6), ((0, 1, 2, 3), (4, 5), (6, 7), (8, 9)))
            gate_coef(1, 2 * C, "g_post_mix")
            run_phase(dve, split, QPROJ, lambda i: None, lambda i: None)

            new_ps = ps[0:64, 0:2, :]
            new_sp = sp_new[:].rearrange("p j a q -> p j (a q)")
            dve.wait_ge(s_const, CONSTS)
            dve.tensor_reduce(out=bsb_row[:], in_=bsb_sel[:], axis=mybir.AxisListType.X, op=ALU.add).then_inc(bias_row, 1)
            dve.wait_ge(new_step, 3)
            dve.tensor_scalar(new_sp, new_sp, EXP_CAP, None, ALU.min).then_inc(new_step, 1)
            dve.wait_ge(new_step, 5)
            dve.tensor_tensor(new_sp, new_ps, new_sp, ALU.max).then_inc(new_step, 1)

            def cap(j, i):
                dve.wait_ge(exped, 2 * i + (j + 1))
                dve.tensor_scalar(att[j][:], att[j][:], EXP_CAP, None, ALU.min).then_inc(capped, 1)

            def softplus(j, i):
                dve.wait_ge(lned, 2 * i + (j + 1))
                dve.scalar_tensor_tensor(out=att[j][:], in0=z_cols(j), scalar=bsb[:, bass.ds(2 * i + j, 1)],
                                         in1=att[j][:], op0=ALU.add, op1=ALU.max).then_inc(sp_done, 1)

            def seq_o_copy(i):
                dve.wait_ge(seq_av, i + 1)
                dve.tensor_copy(o_seq[:], ps[:, 7, 0:2 * P]).then_inc(seq_o_copied, 1)

            def seq_o(i):
                dve.wait_ge(seq_o_turned, i + 1)
                for lo in range(2):
                    if lo:
                        dve.wait_ge(seq_hi_done, i + 1)
                    for j in range(2):
                        r = slice(HD * j, HD * j + HD)
                        src = ps[r, 7, 256:384].rearrange("p (a t h q) -> p t a h q", a=2, h=2, q=TS)[:, :, :, j]
                        hi, low = (h[r, :, bass.ds(i * TS + TP, TS)].rearrange("p (t a) q -> p t a q", a=2)
                                   for h in (h_hi, h_lo))
                        if lo:
                            ins = dve.tensor_tensor(low, src, hi.bitcast(F32), ALU.subtract)
                        else:
                            ins = dve.tensor_copy(hi, src)
                    ins.then_inc(seq_bank_free if lo else seq_hi_done, 1)

            def pair_o(i):
                dve.wait_ge(av_done, 2 * i + 2)
                dve.tensor_copy(chunk(h_hi, i, 0, TP), ps[:, 6, :]).then_inc(pair_hi_done, 1)
                dve.wait_ge(pair_hi_done, i + 1)
                dve.tensor_tensor(chunk(h_lo, i, 0, TP), ps[:, 6, :], chunk(h_hi, i, 0, TP).bitcast(F32), ALU.subtract)\
                    .then_inc(pair_bank_free, 1)

            def rest_of_pair(i):
                cap(1, i)
                dve.wait_ge(seq_exped, i + 1)
                dve.tensor_scalar(att_s[:], att_s[:], EXP_CAP, None, ALU.min).then_inc(seq_capped, 1)
                softplus(1, i)
                dve.wait_ge(seq_lned, i + 1)
                dve.tensor_tensor(att_s[:], ps[:, 7, :], att_s[:], ALU.max).then_inc(seq_sp, 1)

            cap(0, 0)
            softplus(0, 0)
            rest_of_pair(0)
            with dve.Fori(1, PAIRS) as i:
                cap(0, i)
                seq_o_copy(i - 1)
                softplus(0, i)
                seq_o(i - 1)
                pair_o(i - 1)
                rest_of_pair(i)
            seq_o_copy(PAIRS - 1)
            seq_o(PAIRS - 1)
            pair_o(PAIRS - 1)

            y_squares(2, OPROJ, False)
            scale_coef(1, 4 * C, "g_pre_ffn")
            residual(2, 7)
            apply_norm(5, x, 8)
            ffn(1, 3)
            residual(3, 9)

        @block.gpsimd
        def _(pool):
            pool.memset(c_act[:], 0.0).then_inc(pads_ready, 1)
            pool.dma_start(bsb[:], b_sb_in.partition_broadcast(P)).then_inc(s_bsb, 16)
            pool.dma_start(pages[:], page_table).then_inc(s_pages, 16)
            pool.dma_start(u_s[:, :, :, 0:WA - 1].rearrange("p c s t -> p (c s) t"), state_a).then_inc(s_state, 16)
            pool.memset(eps_col[:], EPS).then_inc(s_const, 1)
            pool.memset(no_shift[:], 0.0).then_inc(s_const, 1)
            pool.memset(mean_w[:], 1.0 / D).then_inc(s_const, 1)
            pool.memset(one_row[:], 1.0).then_inc(s_const, 1)
            pool.memset(neg_ones[:], -1.0).then_inc(s_const, 1)
            pool.memset(ident[:], 1.0).then_inc(s_const, 1)
            pool.memset(mask[:], -1e30).then_inc(s_const, 1)
            pool.memset(mask_new[:], 0.0).then_inc(s_const, 1)
            pool.memset(tri[:], -1.0).then_inc(s_const, 1)
            pool.memset(four_diag[:], 1.0).then_inc(s_const, 1)
            pool.wait_ge(s_const, 10)
            pool.affine_select(out=tri[:], in_=tri[:], compare_op=ALU.is_ge, fill=0.0, base=0, pattern=[[-1, P]],
                               channel_multiplier=1).then_inc(s_const, 1)
            pool.affine_select(out=ident[:], in_=ident[:], compare_op=ALU.is_equal, fill=0.0, base=0,
                               pattern=[[-1, P]], channel_multiplier=1).then_inc(s_const, 1)
            pool.affine_select(out=mask[:], in_=mask[:], compare_op=ALU.is_ge, fill=0.0, base=0, pattern=[[-1, P]],
                               channel_multiplier=1).then_inc(s_const, 1)
            pool.affine_select(out=four_diag[:], in_=four_diag[:], compare_op=ALU.is_equal, fill=0.0, base=0,
                               pattern=[[-32, ADA_TILES], [-1, NB]], channel_multiplier=1).then_inc(s_const, 1)
            pool.memset(u_p[:, :, 0:WA - 1], 0.0).then_inc(pads_ready, 1)
            m3 = mask_new[:].rearrange("p (s q) -> p s q", s=NS)
            for n, (base, cm, pattern) in enumerate(((-1, -1, [[TS, NS], [1, TS]]), (0, 1, [[-TS, NS], [0, TS]]),
                                                     (TS - 1, -1, [[TS, NS], [0, TS]]))):
                pool.wait_ge(s_const, 14 + n)
                pool.affine_select(out=m3, in_=m3, compare_op=ALU.is_ge, fill=-1e30, base=base, pattern=pattern,
                                   channel_multiplier=cm).then_inc(s_const, 1)
            pool.wait_ge(s_bsb, 16)
            pool.wait_ge(s_const, 17)
            pool.tensor_copy(bsb_sel[:], bsb[:]).then_inc(s_const, 1)
            pool.wait_ge(s_const, 18)
            pool.affine_select(out=bsb_sel[:], in_=bsb_sel[:], compare_op=ALU.is_ge, fill=0.0, base=0,
                               pattern=[[-TS, HEADS]], channel_multiplier=1).then_inc(s_const, 1)
            pool.wait_ge(s_const, 19)
            pool.affine_select(out=bsb_sel[:], in_=bsb_sel[:], compare_op=ALU.is_ge, fill=0.0, base=TS - 1,
                               pattern=[[TS, HEADS]], channel_multiplier=-1).then_inc(s_const, 1)

            def modulate_seq(norm, shift, at):
                k = {0: 0, 2: 1, 3: 2, 4: 3, 5: 4}[norm]
                for n in range(C):
                    t = seq(hn[:, n % HN, TP:TT])
                    pool.wait_ge(hn_x, norm * C + n + 1)
                    pool.tensor_tensor(t, t, per_seq(a_mod, n), ALU.mult).then_inc(hn_s, 1)
                    pool.wait_ge(hn_s, 2 * (k * C + n) + 1)
                    pool.tensor_tensor(t, t, shift[:, at + n, 1:NB].unsqueeze(2).to_broadcast([P, NS, TS]), ALU.add)\
                        .then_inc(hn_s, 1)

            modulate_seq(0, mod[:, 0], 0)

            pool.memset(u_seq[:], 0.0).then_inc(pads_ready, 1)
            pool.memset(w_seq[:], 0.0).then_inc(pads_ready, 1)
            pool.wait_ge(pads_ready, 4)
            pool.wait_ge(s_state, 16)
            with pool.Fori(0, C) as i:
                def products(part):
                    rows = u_seq[:, :, part * SEQ_PART:part * SEQ_PART + TS]
                    windows = bass.AP(tensor=rows.tensor, offset=rows.offset,
                                      ap=[list(rows.ap[0]), [1, SEQ_PART], list(rows.ap[1]), list(rows.ap[2])])
                    w = w_seq[:, part * SEQ_PART:(part + 1) * SEQ_PART].unsqueeze(2).unsqueeze(3)
                    pool.tensor_tensor((s_prod if part else s_sum)[:], windows,
                                       w.to_broadcast([P, SEQ_PART, NS, TS]), ALU.mult).then_inc(conv_seq, 1)

                def step(n):
                    pool.wait_ge(conv_seq, SEQ_STEPS * i + n)

                pool.wait_ge(slot_free[1], i + 1)
                pool.tensor_copy(u_seq[:, :, 0:WA - 1 + TS], u_s[:, bass.ds(i, 1), :, :].rearrange("p a s t -> p (a s) t"))\
                    .then_inc(conv_seq, 1)
                pool.tensor_copy(w_seq[:, 0:WA], prm("w_a_dw", i * WA, WA)).then_inc(conv_seq, 1)
                pool.tensor_copy(w_seq[:, WA + 1:WA + 2], prm("b_a_dw", i)).then_inc(conv_seq, 1)
                step(3)
                products(0)
                products(1)
                for part in range(1, WA // SEQ_PART + 1):
                    step(2 * part + 3)
                    pool.tensor_tensor(s_sum[:], s_sum[:], s_prod[:], ALU.add).then_inc(conv_seq, 1)
                    if part < WA // SEQ_PART:
                        step(2 * part + 4)
                        products(part + 1)
                for n, half in enumerate((4, 2, 1)):
                    step(2 * (WA // SEQ_PART) + 4 + n)
                    pool.tensor_tensor(s_sum[:, 0:half], s_sum[:, 0:half], s_sum[:, half:2 * half], ALU.add)\
                        .then_inc(conv_seq, 1)
                step(SEQ_STEPS - 1)
                pool.tensor_tensor(seq(chunk(y, i, TP, TT)), s_sum[:, 0],
                                   w_seq[:, WA + 1:WA + 2].unsqueeze(2).to_broadcast([P, NS, TS]), ALU.add)\
                    .then_inc(conv_seq, 1)
                step(SEQ_STEPS)
            pool.dma_start(conv_a_p, u_p[:, :, TP:TP + WA - 1]).then_inc(conv_stored, 16)
            pool.dma_start(conv_a_s, u_s[:, :, :, TS:TS + WA - 1].rearrange("p c s t -> p (c s) t")).then_inc(conv_stored, 16)

            def scale_seq(r, coef):
                pool.wait_ge(coef_ready, coef)
                with pool.Fori(0, C) as i:
                    pool.wait_ge(y_scaled, i + (r * C + 1))
                    t = seq(chunk(y, i, TP, TT))
                    pool.tensor_tensor(t, t, chunk(g_mod, i, 1, NB).unsqueeze(2).to_broadcast([P, NS, TS]), ALU.mult)\
                        .then_inc(y_scaled_s, 1)

            def residual(r, index):
                pool.wait_ge(rs_ready, index + 1)
                pool.wait_ge(y_scaled, r * C + C)
                pool.wait_ge(y_scaled_s, r * C + C)
                for n in range(DVE_CHUNKS, C):
                    pool.tensor_tensor(y[:, n, :], y[:, n, :], rs[:], ALU.mult).then_inc(y_normed_p, 1)
                    pool.wait_ge(y_normed_p, r * (C - DVE_CHUNKS) + n - DVE_CHUNKS + 1)
                    pool.tensor_tensor(x[:, n, :], x[:, n, :], y[:, n, :], ALU.add).then_inc(x_ready_p, 1)

            def ffn(layer, r, coef):
                pool.dma_start(f_state[:], state_f[layer]).then_inc(s_fstate, 16)
                pool.memset(g_pad[:, 0:WF - 1], 0.0).then_inc(pads_ready, 1)
                pool.wait_ge(s_fstate, 16 * (layer + 1))
                g0 = layer * FC

                def save_tail(i):
                    g = i + g0
                    pool.wait_ge(gate_copied, g + 1)
                    t = tails[:, bass.ds(i, 1), :].rearrange("p a t -> p (a t)")
                    pool.tensor_copy(t[:, 0:2], g_pad[:, TP:TP + 2]).then_inc(tail_saved, 1)
                    pool.tensor_copy(t[:, 2:].rearrange("p (s t) -> p s t", t=2), g_seq[:, :, TS:TS + 2])\
                        .then_inc(tail_saved, 1)

                def put_state(i):
                    pool.tensor_copy(g_seq[:, :, 0:2], f_state[:, bass.ds(i, 1), :]
                                     .rearrange("p a (s t) -> p (a s) t", t=2)).then_inc(state_put, 1)

                put_state(0)
                save_tail(0)
                with pool.Fori(1, FC) as i:
                    pool.wait_ge(conv_done, i + g0)
                    put_state(i)
                    save_tail(i)
                pool.wait_ge(tail_saved, 2 * (g0 + FC))
                pool.dma_start(ffn_tails[layer], tails[:]).then_inc(tails_stored, 16)
                scale_seq(r, coef)
                residual(r, 5 if layer == 0 else 9)

            scale_seq(0, 2)
            residual(0, 3)
            modulate_seq(2, mod[:, 0], 3 * C)
            ffn(0, 1, 4)
            modulate_seq(3, no_shift, 0)
            for s in range(2):
                pool.wait_ge(slot_free[s], VPROJ[0] // 2)
            pool.dma_start(k_out, k_t[:]).then_inc(kv_stored, 16)
            modulate_seq(4, mod[:, 1], 0)
            pool.wait_ge(v_act, 6)
            pool.wait_ge(v_dve, 4)
            pool.dma_start(v_out[0:TP].rearrange("(t p) c -> p t c", p=P), v_n[:, 0:4, :]).then_inc(kv_stored, 16)
            pool.dma_start(v_out[TP:TT], v_n[0:TT - TP, 4, :]).then_inc(kv_stored, 16)
            pool.wait_ge(h_ready, 5 * C)
            pool.wait_ge(tails_stored, 16)
            pool.tensor_copy(ident_f[:], ident[:]).then_inc(buffers_free, 1)
            pool.wait_ge(s_lo, OPROJ[0] + 2)
            pool.memset(q_seq[:], 0.0).then_inc(buffers_free, 1)
            for s in range(2):
                pool.wait_ge(slot_free[s], tiles_before(OPROJ[0]))

            def stage_k(j, i):
                r = slice(HD * j, HD * j + HD)
                pool.tensor_copy(k_st[r, :], chunk(k_t, i, 0, TP)[r]).then_inc(k_staged, 1)
                pool.tensor_copy(q_st[r, :], chunk(q_t, i, 0, TP)[r]).then_inc(k_staged, 1)
                pool.wait_ge(k_staged, 4 * i + (2 * j + 2))

            def stage_v(j, i):
                pool.tensor_copy(v_st[:, :, HD * j:HD * j + HD], v_n[:, 0:4, bass.ds(i * P + HD * j, HD)])\
                    .then_inc(v_staged, 1)
                pool.wait_ge(v_staged, 2 * i + (j + 1))

            def stage_q(i):
                for j in range(2):
                    r = slice(HD * j, HD * j + HD)
                    for a in range(2):
                        at = 2 * TS * a + TS * j
                        pool.tensor_copy(q_seq[r, a:PAIRS:2, at:at + TS], q_t[r, a:PAIRS:2, bass.ds(i * TS + TP, TS)])\
                            .then_inc(q_staged, 1)
                    pool.wait_ge(q_staged, 4 * i + (2 * j + 2))

            def stage_new(i):
                pool.tensor_copy(att_st[:].rearrange("p (a j q) -> p j a q", j=2, q=TS), att_new[:, :, :, bass.ds(i * TS, TS)])\
                    .then_inc(new_staged, 1)
                pool.wait_ge(new_staged, i + 1)

            def finish_pair(i):
                pool.wait_ge(seq_av, i + 1)
                for t in range(PAGES):
                    page_load(pool, i + 1, t, v_page, cache_v, v_in)
                stage_new(i + 1)
                pool.wait_ge(av_done, 2 * i + 2)
                stage_v(1, i + 1)

            def rest_of_pair(i):
                pool.wait_ge(k_used, i + 1)
                stage_q(i + 1)
                pool.wait_ge(z_done, 2 * i + 2)
                stage_k(1, i + 1)
                pool.wait_ge(av_done, 2 * i + 1)
                stage_v(0, i + 1)

            pool.wait_ge(s_pages, 16)
            pool.wait_ge(buffers_free, 2)
            stage_k(0, 0)
            stage_k(1, 0)
            stage_q(0)
            stage_v(0, 0)
            stage_v(1, 0)
            for t in range(PAGES):
                page_load(pool, 0, t, v_page, cache_v, v_in)
            pool.wait_ge(new_step, 8)
            stage_new(0)
            pool.wait_ge(z_done, 1)
            stage_k(0, 1)
            rest_of_pair(0)
            with pool.Fori(1, PAIRS - 1) as i:
                pool.wait_ge(z_done, 2 * i + 1)
                stage_k(0, i + 1)
                finish_pair(i - 1)
                rest_of_pair(i)
            finish_pair(PAIRS - 2)
            scale_seq(2, 7)
            residual(2, 7)
            modulate_seq(5, mod[:, 1], 3 * C)
            ffn(1, 3, 9)
            pool.wait_ge(conv_stored, 32)
            pool.wait_ge(kv_stored, 48)
            pool.wait_ge(tails_stored, 32)


_OUTS = [("y_t", (P, C, TT)), ("conv_a_p", (P, C, WA - 1)), ("conv_a_s", (P, C * NS, WA - 1)),
         ("ffn_tails", (DEPTH, P, FC, 2 * NB)), ("k_t", (P, PAIRS, TT)), ("v", (TT, D))]


def _blocks(w, k, cols):
    return w.reshape(k, P, -1, cols).transpose(2, 1, 0, 3).reshape(-1, P, k * cols)


def _features(a):
    a = a.reshape(*a.shape[:-1], -1, P)
    return np.moveaxis(a, -1, 0)


def kernel(**inputs):
    import concourse.bacc as bacc
    from concourse.bass_utils import run_bass_kernel_spmd

    v = {name: np.asarray(a) for name, a in inputs.items()}
    tokens = np.concatenate([v["x_prompt"].reshape(TP, D), v["x_sample"].reshape(NS * TS, D)])
    c_rows = np.concatenate([v["c_prompt"], v["c_sample"]])
    par = np.concatenate(
        [_features(v[n]).reshape(P, -1) for n in ("g_pre_mix", "g_post_mix", "g_pre_ffn", "g_post_ffn", "b_a_dw",
                                                  "ln_a_g", "ln_a_b")]
        + [_features(v["g_kv"]).reshape(P, -1),
           _features(v["w_a_dw"][0]).transpose(0, 2, 1).reshape(P, -1),
           _features(v["b_ffn_dw"]).reshape(P, -1),
           _features(v["w_ffn_dw"]).transpose(0, 1, 3, 2).reshape(P, -1),
           _features(v["b_ada"]).reshape(P, -1)], axis=1)

    def alternate(a, b):
        return np.stack([_blocks(a, C, P), _blocks(b, C, P)], axis=1).reshape(-1, P, C * P)

    def up(layer, hf):
        w, n = v["w_ffn_up"][layer], FH * P
        return alternate(w[:, hf * n:(hf + 1) * n], w[:, FF + hf * n:FF + (hf + 1) * n])

    def wide_units(w):
        return w.reshape(4, 2, P, 2, 512).transpose(3, 0, 2, 1, 4).reshape(8, P, C * P)

    w_in, w_kv = v["w_a_in"][0], v["w_kv"]
    w_k8 = np.concatenate([alternate(w_in[:, D:], w_in[:, :D]), _blocks(v["w_a_out"][0], C, P), up(0, 0), up(0, 1),
                           _blocks(w_kv[:, :D], C, P), wide_units(w_kv[:, D:]), _blocks(v["w_q"][0], C, P),
                           _blocks(v["w_o"][0], C, P), up(1, 0), up(1, 1)])
    w_down = np.concatenate([_blocks(v["w_ffn_down"][layer][hf * FH * P:(hf + 1) * FH * P], FH, P)
                             for layer in range(DEPTH) for hf in range(2)])
    w_ada = v["w_ada"].reshape(DEPTH, C, P, GROUPS // DEPTH, 2, C * P).transpose(0, 3, 1, 4, 2, 5).reshape(-1, P, C * P)
    arrays = {
        "x_in": _features(tokens).transpose(0, 2, 1),
        "c_in": _features(c_rows).transpose(0, 2, 1),
        "par_in": par,
        "b_sb_in": v["b_sb"].reshape(1, HEADS),
        "w_ada": w_ada,
        "w_k8": w_k8,
        "w_down": w_down,
        "state_a": _features(v["state_conv_a"][0]).transpose(0, 3, 1, 2).reshape(P, C * NS, WA - 1),
        "state_f": _features(v["state_ffn_conv"]).transpose(1, 0, 4, 2, 3).reshape(DEPTH, P, FC, NS * (WF - 1)),
        "cache_kt": v["cache_k"].reshape(N_PHYS, PAGE, PAIRS, P).transpose(0, 3, 2, 1).reshape(N_PHYS, P, PAIRS * PAGE),
        "cache_v": v["cache_v"].reshape(N_PHYS, PAGE, D),
        "page_table": v["page_table"].reshape(1, NS * PAGES).astype(np.int32),
    }
    arrays = {name: np.ascontiguousarray(a) for name, a in arrays.items()}
    nc = bacc.Bacc("TRN2", target_bir_lowering=False, num_devices=1)
    args = {name: nc.dram_tensor(f"{name}_dram", a.shape, mybir.dt.from_np(a.dtype), kind="ExternalInput").ap()
            for name, a in arrays.items()}
    outs = {name: nc.dram_tensor(f"{name}_dram", shape, F32, kind="ExternalOutput").ap() for name, shape in
            [(f"{n}_out", s) for n, s in _OUTS]}
    trunk_kernel(nc, *args.values(), *outs.values())
    r = run_bass_kernel_spmd(nc, [{f"{name}_dram": a for name, a in arrays.items()}], core_ids=[0])
    y, ca_p, ca_s, tails, k, val = (r.results[0][f"{n}_out_dram"] for n, _ in _OUTS)

    y = y.transpose(2, 1, 0).reshape(TT, D)
    k = k.transpose(2, 1, 0).reshape(TT, HEADS, HD)
    val = val.reshape(TT, HEADS, HD)
    ca_p = ca_p.transpose(2, 1, 0).reshape(1, 1, WA - 1, D)
    ca_s = ca_s.reshape(P, C, NS, WA - 1).transpose(2, 3, 1, 0).reshape(1, NS, WA - 1, D)
    tails = tails.reshape(DEPTH, P, FC, NB, 2).transpose(0, 3, 4, 2, 1).reshape(DEPTH, NB, 2, FF)
    return (y[:TP].reshape(1, TP, D), y[TP:].reshape(NS, TS, D), ca_p, ca_s, tails[:, :1], tails[:, 1:],
            k[:TP].reshape(1, TP, HEADS, HD), val[:TP].reshape(1, TP, HEADS, HD),
            k[TP:].reshape(NS, TS, HEADS, HD), val[TP:].reshape(NS, TS, HEADS, HD))
```
